# Optimizing a Trainium2 kernel written in Bass

```python
import math
import jax, jax.numpy as jnp
from jax import lax
import numpy as np

D_MODEL = 2048
BATCH = 1
SEQ = 256
DEPTH = 1
DEC_BATCH = 8
DEC_SEQ = 8
PAST_LEN = 256
PAGE_SIZE = 128

F32 = jnp.float32
N_META = 16
RMS_EPS = 1e-6
M_H = 4
M_DK = 128
M_DV = 256
M_CHUNK = 64
F_BIAS_INIT = 3.0
A_H = 8
A_DH = 128
IDX_H = 16
IDX_D = 64
TOPK_MAX = 256
Q_BLOCK = 128
REL_BUCKETS = 32
REL_MAX_DIST = 128
PEER_H = 8
PEER_DQ = 256
N_KEYS = 128
N_EXPERTS = N_KEYS * N_KEYS
PEER_TOPK = 16
PEER_BLOCK = 128
IN_SPLITS = (M_H * M_DK, M_H * M_DK, M_H * M_DV, M_H * M_DV, M_H, M_H,
             A_H * A_DH, A_H * A_DH, A_H * A_DH, IDX_H * IDX_D, IDX_D, IDX_H)
P_IN = sum(IN_SPLITS)
MIX = M_H * M_DV + A_H * A_DH

kernel_name = 'mlstm_dsa_peer_hybrid_step'

def rmsnorm(x, g):
    xf = x.astype(F32)
    y = xf * lax.rsqrt(jnp.mean(xf * xf, axis=-1, keepdims=True) + RMS_EPS)
    return (y * g.astype(F32)).astype(x.dtype)

def mixer_inputs(hn, w_in, b_i, b_f):
    B, T, _ = hn.shape
    cuts = np.cumsum(IN_SPLITS)[:-1].tolist()
    mq, mk, mv, mo, ig, fg, aq, ak, av, iq, ik, iw = jnp.split(hn @ w_in, cuts, axis=-1)

    def heads(a, d):
        return a.reshape(B, T, M_H, d).transpose(0, 2, 1, 3).astype(F32)

    li = (ig + b_i).astype(F32).transpose(0, 2, 1)
    lf = jax.nn.log_sigmoid((fg + b_f).astype(F32)).transpose(0, 2, 1)
    m_in = (heads(mq, M_DK), heads(mk, M_DK) * (M_DK ** -0.5), heads(mv, M_DV), li, lf)
    dsa_in = (aq.reshape(B, T, A_H, A_DH), ak.reshape(B, T, A_H, A_DH), av.reshape(B, T, A_H, A_DH),
              iq.reshape(B, T, IDX_H, IDX_D), ik, iw)
    return m_in, mo, dsa_in

def mlstm_chunk(carry, inp):
    C, n, m = carry
    q, k, v, li, lf = inp
    L = q.shape[2]
    b = jnp.cumsum(lf, axis=-1)
    causal = jnp.tril(jnp.ones((L, L), dtype=bool))
    dmat = jnp.where(causal, b[..., :, None] - b[..., None, :] + li[..., None, :], -jnp.inf)
    inter = b + m[..., None]
    m_t = jnp.maximum(inter, jnp.max(dmat, axis=-1))
    w_inter = jnp.exp(inter - m_t)
    s = jnp.einsum('bhtd,bhsd->bhts', q, k) * jnp.exp(dmat - m_t[..., None])
    num = w_inter[..., None] * jnp.einsum('bhtd,bhde->bhte', q, C) + jnp.einsum('bhts,bhse->bhte', s, v)
    den = w_inter * jnp.einsum('bhtd,bhd->bht', q, n) + jnp.sum(s, axis=-1)
    h = num / jnp.maximum(jnp.abs(den), jnp.exp(-m_t))[..., None]
    b_last = b[..., -1]
    g = b_last[..., None] - b + li
    m_new = jnp.maximum(b_last + m, jnp.max(g, axis=-1))
    a = jnp.exp(b_last + m - m_new)
    wk = jnp.exp(g - m_new[..., None])
    C_new = a[..., None, None] * C + jnp.einsum('bhs,bhsd,bhse->bhde', wk, k, v)
    n_new = a[..., None] * n + jnp.einsum('bhs,bhsd->bhd', wk, k)
    return (C_new, n_new, m_new), h

def mlstm_scan(carry, inp):
    T = inp[0].shape[2]
    nc = T // M_CHUNK

    def to_chunks(a):
        return jnp.moveaxis(a.reshape(a.shape[:2] + (nc, M_CHUNK) + a.shape[3:]), 2, 0)

    carry, hs = lax.scan(mlstm_chunk, carry, tuple(to_chunks(a) for a in inp))
    h = jnp.moveaxis(hs, 0, 2)
    return carry, h.reshape(h.shape[:2] + (T, M_DV))

def t5_bias(rel, table):
    max_exact = REL_BUCKETS // 2
    nf = jnp.maximum(rel, 1).astype(F32)
    large = max_exact + (jnp.log(nf / max_exact) / math.log(REL_MAX_DIST / max_exact)
                         * (REL_BUCKETS - max_exact)).astype(jnp.int32)
    large = jnp.minimum(large, REL_BUCKETS - 1)
    bucket = jnp.where(rel < max_exact, rel, large)
    return table[bucket]

def dsa_attend(q, qi, wi, q_pos, k_all, v_all, ki_all, rel_table, topk):
    S = k_all.shape[1]
    key_pos = jnp.arange(S, dtype=jnp.int32)
    dots = jax.nn.relu(jnp.einsum('bthd,bsd->bths', qi.astype(F32), ki_all.astype(F32)))
    score = jnp.einsum('bth,bths->bts', wi.astype(F32) * (IDX_D ** -0.5 * IDX_H ** -0.5), dots)
    causal = key_pos[None, :] <= q_pos[:, None]
    score = jnp.where(causal[None], score, -jnp.inf)
    _, idx = lax.top_k(score, topk)
    valid = idx <= q_pos[None, :, None]
    gather = jax.vmap(lambda rows, ids: rows[ids])
    k_sel = gather(k_all, idx).astype(F32)
    v_sel = gather(v_all, idx).astype(F32)
    logits = jnp.einsum('bthd,btjhd->bhtj', q.astype(F32), k_sel) * (A_DH ** -0.5)
    bias = t5_bias(jnp.maximum(q_pos[None, :, None] - idx, 0), rel_table.astype(F32))
    logits = jnp.where(valid[:, None], logits + bias.transpose(0, 3, 1, 2), -jnp.inf)
    p = jax.nn.softmax(logits, axis=-1)
    return jnp.einsum('bhtj,btjhd->bthd', p, v_sel).astype(q.dtype)

def dsa_prompt_blocks(q, qi, wi, q_pos, k_all, v_all, ki_all, rel_table, topk):
    B, Tq = q.shape[:2]
    nb = Tq // Q_BLOCK

    def blk(a):
        return jnp.moveaxis(a.reshape((B, nb, Q_BLOCK) + a.shape[2:]), 1, 0)

    def one(args):
        qb, qib, wib, pb = args
        return dsa_attend(qb, qib, wib, pb, k_all, v_all, ki_all, rel_table, topk)

    out = lax.map(one, (blk(q), blk(qi), blk(wi), q_pos.reshape(nb, Q_BLOCK)))
    return jnp.moveaxis(out, 0, 1).reshape(q.shape)

def mixer_output(h_m, mo, attn, mh_g, w_out):
    B, H, T, DV = h_m.shape
    hm = h_m * lax.rsqrt(jnp.mean(h_m * h_m, axis=-1, keepdims=True) + RMS_EPS)
    hm = hm.transpose(0, 2, 1, 3).reshape(B, T, H * DV) * mh_g.astype(F32) * jax.nn.sigmoid(mo.astype(F32))
    mixed = jnp.concatenate([hm.astype(mo.dtype), attn.reshape(B, T, A_H * A_DH).astype(mo.dtype)], axis=-1)
    return mixed @ w_out

def peer_block(x, wq, k1, k2, U, V):
    N = x.shape[0]
    qq = (x @ wq).reshape(N, PEER_H, 2, PEER_DQ // 2).astype(F32)
    s1 = jnp.einsum('nhd,hkd->nhk', qq[:, :, 0], k1.astype(F32))
    s2 = jnp.einsum('nhd,hkd->nhk', qq[:, :, 1], k2.astype(F32))
    v1, i1 = lax.top_k(s1, PEER_TOPK)
    v2, i2 = lax.top_k(s2, PEER_TOPK)
    cand = (v1[..., :, None] + v2[..., None, :]).reshape(N, PEER_H, PEER_TOPK * PEER_TOPK)
    sc, ci = lax.top_k(cand, PEER_TOPK)
    e = (jnp.take_along_axis(i1, ci // PEER_TOPK, axis=-1) * N_KEYS
         + jnp.take_along_axis(i2, ci % PEER_TOPK, axis=-1))
    g = jax.nn.softmax(sc, axis=-1)
    act = jax.nn.gelu(jnp.einsum('nd,nhjd->nhj', x.astype(F32), U[e].astype(F32)), approximate=False)
    out = jnp.einsum('nhj,nhjd->nd', g * act, V[e].astype(F32))
    return out.astype(x.dtype)

def peer(x, wq, k1, k2, U, V):
    B, T, D = x.shape
    n = B * T
    pad = (-n) % PEER_BLOCK
    blocks = jnp.pad(x.reshape(n, D), ((0, pad), (0, 0))).reshape(-1, PEER_BLOCK, D)
    out = lax.map(lambda xb: peer_block(xb, wq, k1, k2, U, V), blocks)
    return out.reshape(-1, D)[:n].reshape(B, T, D)

def paged_rows(pool, page_table):
    g = pool[page_table]
    return g.reshape((g.shape[0], g.shape[1] * g.shape[2]) + g.shape[3:])

def setup_inputs(seed: int = 0) -> dict:
    key = jax.random.key(seed)
    ks = jax.random.split(key, 24)
    n_pages = PAST_LEN // PAGE_SIZE
    n_used = DEC_BATCH * n_pages
    n_pool = n_used + max(1, n_used // 4)

    def nrm(k, shape, s):
        return jax.random.normal(k, shape, F32) * s

    page_table = jax.random.permutation(ks[8], n_pool)[:n_used].reshape(DEC_BATCH, n_pages).astype(jnp.int32)
    return {
        'x_prompt': nrm(ks[0], (BATCH, SEQ, D_MODEL), 1.0),
        'x_sample': nrm(ks[1], (DEC_BATCH, DEC_SEQ, D_MODEL), 1.0),
        'cache_k': nrm(ks[2], (DEPTH, n_pool, PAGE_SIZE, A_H, A_DH), 1.0),
        'cache_v': nrm(ks[3], (DEPTH, n_pool, PAGE_SIZE, A_H, A_DH), 1.0),
        'cache_kidx': nrm(ks[4], (DEPTH, n_pool, PAGE_SIZE, IDX_D), 1.0),
        'state_C': nrm(ks[5], (DEPTH, DEC_BATCH, M_H, M_DK, M_DV), 0.1),
        'state_n': nrm(ks[6], (DEPTH, DEC_BATCH, M_H, M_DK), 0.1),
        'state_m': nrm(ks[7], (DEPTH, DEC_BATCH, M_H), 1.0),
        'page_table': page_table,
        'meta_tokens': nrm(ks[9], (N_META, D_MODEL), 1.0),
        'rel_bias': nrm(ks[10], (REL_BUCKETS, A_H), 0.5),
        'final_norm_g': 1.0 + nrm(ks[11], (D_MODEL,), 0.02),
        'norm1_g': 1.0 + nrm(ks[12], (DEPTH, D_MODEL), 0.02),
        'w_in': nrm(ks[13], (DEPTH, D_MODEL, P_IN), D_MODEL ** -0.5),
        'b_i': nrm(ks[14], (DEPTH, M_H), 0.1),
        'b_f': F_BIAS_INIT + nrm(ks[15], (DEPTH, M_H), 0.1),
        'mh_norm_g': 1.0 + nrm(ks[16], (DEPTH, M_H * M_DV), 0.02),
        'w_out': nrm(ks[17], (DEPTH, MIX, D_MODEL), MIX ** -0.5),
        'norm2_g': 1.0 + nrm(ks[18], (DEPTH, D_MODEL), 0.02),
        'peer_wq': nrm(ks[19], (DEPTH, D_MODEL, PEER_H * PEER_DQ), D_MODEL ** -0.5),
        'peer_k1': nrm(ks[20], (DEPTH, PEER_H, N_KEYS, PEER_DQ // 2), (PEER_DQ // 2) ** -0.5),
        'peer_k2': nrm(ks[21], (DEPTH, PEER_H, N_KEYS, PEER_DQ // 2), (PEER_DQ // 2) ** -0.5),
        'peer_u': nrm(ks[22], (DEPTH, N_EXPERTS, D_MODEL), D_MODEL ** -0.5),
        'peer_v': nrm(ks[23], (DEPTH, N_EXPERTS, D_MODEL), PEER_H ** -0.5),
    }

def reference(x_prompt, x_sample, cache_k, cache_v, cache_kidx, state_C, state_n, state_m, page_table,
              meta_tokens, rel_bias, final_norm_g, norm1_g, w_in, b_i, b_f, mh_norm_g, w_out, norm2_g,
              peer_wq, peer_k1, peer_k2, peer_u, peer_v):
    B, S_p, _ = x_prompt.shape
    Bs, Ts, _ = x_sample.shape
    past = page_table.shape[1] * PAGE_SIZE
    topk_p = min(TOPK_MAX, S_p // 4)
    topk_s = min(TOPK_MAX, (past + Ts) // 4)
    T = N_META + S_p
    pos_p = jnp.arange(T, dtype=jnp.int32)
    pos_s = past + jnp.arange(Ts, dtype=jnp.int32)
    meta = jnp.broadcast_to(meta_tokens.astype(x_prompt.dtype)[None], (B, N_META, D_MODEL))
    hp = jnp.concatenate([meta, x_prompt], axis=1)
    hs = x_sample
    kp, vp, ip, cp, np_, mp = [], [], [], [], [], []
    ks_, vs_, is_, cs_, ns_, ms_ = [], [], [], [], [], []
    for l in range(DEPTH):
        m_in, mo, (aq, ak, av, iq, ik, iw) = mixer_inputs(rmsnorm(hp, norm1_g[l]), w_in[l], b_i[l], b_f[l])
        carry = (jnp.zeros((B, M_H, M_DK, M_DV), F32), jnp.zeros((B, M_H, M_DK), F32), jnp.zeros((B, M_H), F32))
        carry, hm_meta = mlstm_chunk(carry, tuple(a[:, :, :N_META] for a in m_in))
        carry, hm_real = mlstm_scan(carry, tuple(a[:, :, N_META:] for a in m_in))
        attn_real = dsa_prompt_blocks(aq[:, N_META:], iq[:, N_META:], iw[:, N_META:], pos_p[N_META:],
                                      ak, av, ik, rel_bias, topk_p)
        if l == DEPTH - 1:
            hp = hp[:, N_META:] + mixer_output(hm_real, mo[:, N_META:], attn_real, mh_norm_g[l], w_out[l])
        else:
            attn_meta = dsa_attend(aq[:, :N_META], iq[:, :N_META], iw[:, :N_META], pos_p[:N_META],
                                   ak[:, :N_META], av[:, :N_META], ik[:, :N_META], rel_bias, N_META)
            hp = hp + mixer_output(jnp.concatenate([hm_meta, hm_real], axis=2), mo,
                                   jnp.concatenate([attn_meta, attn_real], axis=1), mh_norm_g[l], w_out[l])
        hp = hp + peer(rmsnorm(hp, norm2_g[l]), peer_wq[l], peer_k1[l], peer_k2[l], peer_u[l], peer_v[l])
        kp.append(ak)
        vp.append(av)
        ip.append(ik)
        cp.append(carry[0])
        np_.append(carry[1])
        mp.append(carry[2])
        m_in_s, mo_s, (aq_s, ak_s, av_s, iq_s, ik_s, iw_s) = mixer_inputs(rmsnorm(hs, norm1_g[l]), w_in[l], b_i[l], b_f[l])
        carry_s = (state_C[l].astype(F32), state_n[l].astype(F32), state_m[l].astype(F32))
        carry_s, hm_s = mlstm_chunk(carry_s, m_in_s)
        k_all = jnp.concatenate([paged_rows(cache_k[l], page_table).astype(ak_s.dtype), ak_s], axis=1)
        v_all = jnp.concatenate([paged_rows(cache_v[l], page_table).astype(av_s.dtype), av_s], axis=1)
        ki_all = jnp.concatenate([paged_rows(cache_kidx[l], page_table).astype(ik_s.dtype), ik_s], axis=1)
        attn_s = dsa_attend(aq_s, iq_s, iw_s, pos_s, k_all, v_all, ki_all, rel_bias, topk_s)
        hs = hs + mixer_output(hm_s, mo_s, attn_s, mh_norm_g[l], w_out[l])
        hs = hs + peer(rmsnorm(hs, norm2_g[l]), peer_wq[l], peer_k1[l], peer_k2[l], peer_u[l], peer_v[l])
        ks_.append(ak_s)
        vs_.append(av_s)
        is_.append(ik_s)
        cs_.append(carry_s[0])
        ns_.append(carry_s[1])
        ms_.append(carry_s[2])
    y_prompt = rmsnorm(hp, final_norm_g)
    y_sample = rmsnorm(hs, final_norm_g)
    return (y_prompt, y_sample,
            jnp.stack(kp), jnp.stack(vp), jnp.stack(ip), jnp.stack(cp), jnp.stack(np_), jnp.stack(mp),
            jnp.stack(ks_), jnp.stack(vs_), jnp.stack(is_), jnp.stack(cs_), jnp.stack(ns_), jnp.stack(ms_))


_drawn_inputs = setup_inputs


def setup_inputs(seed=0):
    import zlib

    import numpy as np

    out = dict(_drawn_inputs(seed))
    spreads = {}
    factors = {'final_norm_g': 8.423, 'b_f': 8.0, 'mh_norm_g': 3.107, 'norm2_g': 3.274}
    for name, (base, spread) in spreads.items():
        noise = np.random.default_rng([zlib.crc32(name.encode()), seed]).standard_normal(out[name].shape)
        drawn = base * np.exp(spread * noise) if base else spread * noise
        out[name] = __import__('jax').numpy.asarray(drawn.astype(out[name].dtype))
    for name, factor in factors.items():
        out[name] = (out[name] * factor).astype(out[name].dtype)
    return out
```

```python
from contextlib import ExitStack

import numpy as np

import concourse.bass as bass
from concourse import mybir

ALU = mybir.AluOpType
ACT = mybir.ActivationFunctionType
F32 = mybir.dt.float32
I32 = mybir.dt.int32
U32 = mybir.dt.uint32
FR = mybir.dt.float32r
AX_X = mybir.AxisListType.X

P = 128
D = 2048
KC = D // P
META, SEQ, SB, ST = 16, 256, 8, 8
TP = META + SEQ
TS = SB * ST
T = TP + TS
N = SEQ + TS
MH, DK, DV = 4, 128, 256
AH, DH = 8, 128
IH, ID = 16, 64
TOPK_P = 64
PAST, PAGE = 256, 128
TOPK_S = (PAST + ST) // 4
KS = PAST + ST
NK = 128
PH, PK = 8, 16
BUCKETS = 32
EPS = 1e-6
NEG = -1.0e30
GONE = -3.0e38
C_MQ, C_MK, C_MV, C_MO = 0, 512, 1024, 2048
C_IG, C_FG = 3072, 3076
C_AQ, C_AK, C_AV, C_IQ, C_IK, C_IW = 3080, 4104, 5128, 6152, 7176, 7240
J_MQ, J_MK, J_MV, J_MO, J_AQ, J_AK, J_AV, J_IQ = 0, 4, 8, 16, 24, 32, 40, 48
NJ = 56
NAT = [(0, 128), (128, 128), (256, 16), (TP, TS)]
XTILES = [(0, 128), (128, 128), (256, 80)]
NTILES = [(0, 128), (128, 128), (256, 64)]
BTW = 400
RW = 528
IG = 32
NG = NK // IG
NS = 4
NB = 5
HS = 4
VS = 4
LD = 256
SMALL_LOADS = 11


def bucket_of(rel):
    rel = np.maximum(rel, 0)
    half = BUCKETS // 2
    nf = np.maximum(rel, 1).astype(np.float32)
    scale = np.float32(np.log(128 / half))
    large = half + (np.log(nf / np.float32(half)).astype(np.float32) / scale * np.float32(BUCKETS - half)).astype(np.int32)
    return np.where(rel < half, rel, np.minimum(large, BUCKETS - 1))


def constants():
    p = np.arange(P)
    out = {}
    out["ident"] = np.eye(P)
    out["ones"] = np.ones((P, P))
    out["iota"] = np.tile(np.arange(P), (P, 1))
    s = np.arange(TP)
    out["causal_p"] = np.stack([np.where(s[None] <= META + 128 * i + p[:, None], 0, NEG) for i in range(2)], 1).reshape(P, -1)
    t = META + np.arange(SEQ)
    out["decay_p"] = np.stack([np.where(c + p[:, None] <= t[None], 0, NEG) for c, _ in NAT[:3]], 1).reshape(P, -1)
    r = np.arange(TS)
    same = r[:, None] // ST == r[None] // ST
    out["decay_s"] = np.where(same & (r[:, None] <= r[None]), 0, NEG)
    ks = np.arange(KS)
    out["causal_s"] = np.where(ks[None] <= PAST + (r % ST)[:, None], 0, NEG)
    out["head_row"] = (np.arange(MH)[:, None, None] == np.arange(MH)[None, :, None]).repeat(P, 2).reshape(MH, -1)
    out["spread_h"] = np.arange(IH)[:, None] == (p // ST)[None]
    out["same_t"] = (p % ST)[:, None] == np.tile(np.arange(ST), SB)[None]
    ht = np.arange(AH * ST)
    out["pick_b"] = ((r // ST)[:, None, None] == np.arange(SB)[None, :, None]) & ((r % ST)[:, None, None] == (ht % ST)[None, None])
    out["pick_b"] = out["pick_b"].reshape(TS, -1)
    out["flip"] = np.eye(P)[::-1]
    out["flip_t"] = np.kron(np.eye(AH), np.eye(ST)[::-1])
    out["bucket_hot"] = np.arange(BUCKETS)[:, None] == bucket_of(271 - np.arange(RW))[None]
    at, packed, col = {}, [], 0
    for name, a in out.items():
        at[name] = (col, a.shape)
        packed.append(np.pad(a.astype(np.float32), ((0, P - a.shape[0]), (0, 0))))
        col += a.shape[1]
    return at, np.concatenate(packed, 1)


def plan_jobs():
    jobs = []
    for i in range(3):
        jobs += [("x", i, q) for q in range(KC // 4)]
    jobs += [("gcols",), ("norm1",)]
    jobs += [("gate", 0), ("gate", 1), ("ik",), ("iw",), ("natki",)]
    jobs += [("nat", i, q) for i in range(4) for q in range(7)]
    jobs += [("cols",), ("wcol",), ("n0",), ("bias", 0), ("bias", 1)]
    for h in range(MH):
        jobs += [("mR", h)] + [("mS", h, j) for j in range(3)]
        jobs += [("mN", h, 0), ("mN", h, 1), ("mC", h)]
        jobs += [("mT", h, 0), ("mT", h, 1)]
    for h in range(MH):
        jobs += [("sR", h), ("sW", h), ("sS", h), ("sN", h), ("sT", h)]
        jobs += [("sC", h, b) for b in range(SB)]
    jobs += [("nout",)]
    jobs += [("bt", h) for h in range(AH)] + [("bs",)]
    for i in range(2):
        jobs += [("ix", i, h) for h in range(IH)]
        for h in range(AH + 1):
            jobs += [("aL", i, h)] if h < AH else []
            jobs += [("aP", i, h - 1), ("aO", i, h - 1)] if h else []
    jobs += [("wrep",)]
    for b in range(SB):
        jobs += [("cki", b), ("sI", b)]
    jobs += [("sScore",)]
    for b in range(SB):
        jobs += [("sK", b, q) for q in range(4)]
        jobs += [("sL", b), ("sP", b), ("sO", b)]
    jobs += [("k12", q) for q in range(4)]
    jobs += [("norm2",)]
    for i in range(3):
        jobs += [("pS", i, q) for q in range(4)]
    jobs += [("slots", i) for i in range(3)]
    jobs += [("norm3",)]
    jobs += [("y", i, q) for i in range(3) for q in range(KC // 4)]
    return {k: n for n, k in enumerate(jobs)}


def build(nc, a, o, consts, const_at):
    JOB = plan_jobs()
    ctx = ExitStack()
    base = 16512

    def at(name, offset, shape, dt=F32):
        return nc.alloc_sbuf_tensor_at(name, shape, dt, offset=base + offset, align_bytes=4)

    def sem(name):
        return ctx.enter_context(nc.semaphore(name))

    def tiles(eng, step):
        for n in range(2):
            step(n, n, n // 2)
        with eng.Fori(0, (IG - 8) // 6) as i:
            for r_ in range(6):
                step(i * 6 + (2 + r_), 2 + r_, i * 3 + (2 + r_) // 2)
        for n in range(IG - 6, IG):
            step(n, n, n // 2)

    U_DR, V_DR = a["peer_u"][0], a["peer_v"][0]

    def tail_sync(sp, out, load_weights):
        for q in range(SB):
            evacuated(sp, ("sO", q))
        load_weights(2)
        for n, name in enumerate(("peer_k1", "peer_k2")):
            sp.dma_start(knat[n][:], a[name][0].rearrange("h k d -> k h d")).then_inc(S["knat_in"], 16)
        load_weights(3)
        for i in range(3):
            evacuated(sp, ("slots", i))
        for g in range(NG):
            if g:
                sp.wait_ge(S["v_lo"], 8 + 128 * g)
            with sp.Fori(0, IG // 2) as i:
                for u in range(2):
                    sp.wait_ge(S["u_turned"], i * 2 + (IG * g + u + 1))
                    rows_ = U_DR[bass.ds(i * (2 * P) + (IG * g + u) * P, P), :].rearrange("(g e) (q j) -> q e g j", g=4, q=4)
                    for q in range(4):
                        sp.dma_start(unat[u][32 * q:32 * q + 32], rows_[q]).then_inc(S[f"u_in{u}"], 16)
            sp.wait_ge(S["u_turned"], 2 + IG * (g + 1))
            for s in range(NS):
                with sp.Fori(0, IG // 8) as i:
                    for u in range(2):
                        sp.wait_ge(S["v_lo"], i * 8 + (8 * (IG // 8) * (NS * g + s) + 4 * u + 4))
                        for t in range(4):
                            rows_ = V_DR[bass.ds(i * (8 * P) + (IG * g + 4 * u + t) * P, P), :].rearrange("e (q c) -> e q c", q=4)
                            sp.dma_start(vnat[u][:, t], rows_[:, :, P * s:P * s + P]).then_inc(S[f"vr_in{u}"], 16)
        for i, (c, w) in enumerate(NTILES):
            for q in range(4):
                evacuated(sp, ("y", i, q))
            dst = o["y_prompt"][0][c:c + w] if i < 2 else o["y_sample"].rearrange("b t d -> (b t) d")
            out(dst, ynat[i][0:w, :])

    def tail_tensor(pe, open_bank, close, flip, norm_sum, weight_loop, loop_read):
        banks_idle(pe, ("sO", SB - 1))
        weight_loop(2, mixT)
        loop_read(2)
        for q in range(4):
            b = open_bank(("k12", q))
            pe.wait_ge(S["knat_in"], 32)
            for n in range(4):
                c = 4 * q + n
                mm = flip(b[:, n * P:(n + 1) * P], knat[c % 2][:, c // 2, :], P)
            close(mm)
        norm_sum(("norm2",), 1, N, squares2)
        banks_idle(pe, ("norm2",), range(4))
        pe.wait_ge(S["x2l_done"], KC)
        weight_loop(3, (x2h, x2l))
        loop_read(3)
        for i, (c, w) in enumerate(NTILES):
            for q in range(4):
                b = open_bank(("pS", i, q))
                for n in range(4):
                    k = 4 * q + n
                    evacuated(pe, ("k12", q))
                    mm = pe.matmul(b[0:w, n * P:(n + 1) * P], qqT[:, k, c:c + w], kT12[:, k, :], start=True, stop=True)
                close(mm)
        for i, (c, w) in enumerate(NTILES):
            b = open_bank(("slots", i))
            pe.wait_ge(S["slots_done"], i + 1)
            for n in range(3):
                mm = flip(b[:, n * P:n * P + w], slot[i % 2][0:w, n, :], w)
            close(mm)
        banks_idle(pe, ("slots", 2))

        def one_hot_batch(m, z, banks):
            pe.wait_ge(S["ab_ready"], m + 1)
            pe.wait_ge(S["g_evac"], m + (HS + 1 - banks))
            b = bank[8 - banks + z % banks]
            for n in range(NB):
                mm = pe.matmul(b[:, n * IG:(n + 1) * IG], hot2[z][:, n, :], hot1[z][:, n, :], start=True, stop=True)
            mm.then_inc(S["g_mm"], 1)

        pe.sem_inc(S["act_mm"], 2)
        pe.sem_inc(S["v_mm"], VS)
        pe.sem_inc(S["g_mm"], HS)
        with pe.Fori(0, N // NB // HS) as i:
            for h in range(HS):
                one_hot_batch(i * HS + h, h, HS)
        for g in range(NG):
            def activate(n, r_, pair):
                u, low = r_ % 2, ul[r_ % 3]
                pe.wait_ge(S["u_lo"], n + (IG * g + 1))
                pe.wait_ge(S["a_done"], n + (IG * g + 1))
                for k in range(KC):
                    pe.matmul(bank[4 + u][:, 0:N], uh[u][:, k, :], x2h[:, k, :], start=(k == 0), stop=False)
                    pe.matmul(bank[4 + u][:, 0:N], uh[u][:, k, :], x2l[:, k, :], start=False, stop=False)
                    mm = pe.matmul(bank[4 + u][:, 0:N], low[:, k, :], x2h[:, k, :], start=False, stop=(k == KC - 1))
                mm.then_inc(S["act_mm"], 1)

            tiles(pe, activate)
            for s in range(NS):
                first = NS * g + s
                pe.wait_ge(S["swept"], first) if first else None
                pe.wait_ge(S["zero_set"], 1)
                for d in range(4):
                    pe.matmul(bank[d][:, 0:N], zero[:], x2h[:, 0, :], start=True, stop=False, skip_group_check=True)
                with pe.Fori(0, IG // 8) as i:
                    for e in range(8):
                        u = e % VS
                        pe.wait_ge(S["v_lo"], i * 8 + (IG * first + e + 9))
                        pe.wait_ge(S["al_done"], i * 8 + (IG * first + e + 1))
                        for d in range(4):
                            vh_, vl_ = vh[u][:, d, :], vl[u][:, d, :]
                            pe.matmul(bank[d][:, 0:N], vh_, ah[u][:], start=False, stop=False, skip_group_check=True)
                            pe.matmul(bank[d][:, 0:N], vh_, al[u][:], start=False, stop=False, skip_group_check=True)
                            mm = pe.matmul(bank[d][:, 0:N], vl_, ah[u][:], start=False, stop=False, skip_group_check=True)
                        mm.then_inc(S["v_mm"], 1)
                        if e % 2 and g + 1 < NG:
                            h = e // 2
                            one_hot_batch(i * 4 + (64 * (g + 1) + 16 * s + h), h, 2)
                for d in range(4):
                    mm = pe.matmul(bank[d][:, 0:N], zero[:], x2h[:, 0, :], start=False, stop=True, skip_group_check=True)
                mm.then_inc(S["sweep_mm"], 1)
        pe.wait_ge(S["swept"], NG * NS)
        pe.wait_ge(S["a_done"], 2 + IG * NG)
        norm_sum(("norm3",), 2, N, squares2)
        pe.wait_ge(S["yT_done"], KC)
        for i, (c, w) in enumerate(NTILES):
            for q in range(4):
                b = open_bank(("y", i, q))
                for n in range(4):
                    mm = flip(b[0:w, n * P:(n + 1) * P], yT[:, 4 * q + n, c:c + w], P)
                close(mm)

    def y_view(i, w, q):
        return ynat[i][0:w, :].rearrange("n (q b d) -> n b q d", q=4, d=32)[:, 4 * q:4 * q + 4, :, :]

    def tail_scalar(act, link, square_all, root, loop_copy):
        act.sem_inc(S["g_evac"], HS)
        for q in range(SB):
            evacuated(act, ("sO", q))
        with act.Fori(0, 4) as i:
            for s in range(2):
                act.wait_ge(S[f"w_in{s}"], (i + (w_first[2] + 1)) * 64)
                act.wait_ge(S["proj_mm"], (i + w_first[2]) * 4 + 2 * (s + 1))
                nc.scalar.copy(wperm[s][:].rearrange("p k (c q d) -> p k c q d", c=2, q=4),
                               wring[s][:].rearrange("p k (q c d) -> p k c q d", c=2, q=4)).then_inc(S["wp_done"], 1)
        for q in range(4):
            b = take(act, ("k12", q))
            give(nc.scalar.copy(kT12[:, 4 * q:4 * q + 4, :], b[:].rearrange("p (n w) -> p n w", n=4)), ("k12", q))
        act.wait_ge(S["proj_lo"], 2 + 2 * 18)
        act.wait_ge(S["proj_hi"], 2 + 2 * 18)
        square_all(1, h1T, squares2, lambda c: None)
        root(("norm2",), 1, N)
        for k in range(KC):
            act.wait_ge(S["x2_done"], k + 1)
            nc.scalar.copy(x2h[:, k, :], x2[:, k, :]).then_inc(S["x2h_done"], 1)
        loop_copy(3, qqT)
        for i, (c, w) in enumerate(NTILES):
            if i == 2:
                act.wait_ge(S["cand_done"], 1)
            for q in range(4):
                b = take(act, ("pS", i, q))
                give(nc.scalar.copy(sc[i % 2][0:w, 4 * q:4 * q + 4, :], b[0:w, :].rearrange("p (n w) -> p n w", n=4)), ("pS", i, q))
            act.wait_ge(S["best_done"], i + 1)
            nc.scalar.activation(gate[i % 2][0:w], gate[i % 2][0:w], ACT.Exp).then_inc(S["gate_exp"], 1)
        for i, (c, w) in enumerate(NTILES):
            b = take(act, ("slots", i))
            nc.scalar.copy(i1T[:, c:c + w], b[:, 0:w])
            nc.scalar.copy(i2T[:, c:c + w], b[:, P:P + w])
            give(nc.scalar.copy(gT[:, c:c + w], b[:, 2 * P:2 * P + w]), ("slots", i))

        def spread_out(m, n0_, b, buf):
            act.wait_ge(S["g_mm"], m + (HS + 1))
            nc.scalar.copy(gates[:, buf, :, bass.ds(n0_, NB)], b[:, 0:NB * IG].rearrange("p (n i) -> p i n", n=NB)).then_inc(S["g_evac"], 1)

        with act.Fori(0, N // NB // HS) as i:
            for h in range(HS):
                spread_out(i * HS + h, i * (HS * NB) + NB * h, bank[8 - HS + h], 0)
        for g in range(NG):
            if g:
                act.wait_ge(S["v_mm"], VS + 128 * g)

            def high(n, r_):
                act.wait_ge(S["u_turned"], n + (IG * g + 3))
                act.wait_ge(S["act_mm"], n + (IG * g + 1))
                nc.scalar.copy(uh[r_ % 2][:], ut[r_ % 3][:]).then_inc(S["u_hi"], 1)

            def gelu(n, r_):
                act.wait_ge(S["act_mm"], n + (IG * g + 3))
                nc.scalar.activation(bank[4 + r_ % 2][:, 0:N], bank[4 + r_ % 2][:, 0:N], ACT.Gelu).then_inc(S["gelu_done"], 1)

            def high_gelu(n, r_, pair):
                high(n, r_)
                if r_ >= 2:
                    gelu(n - 2, r_ - 2)

            tiles(act, high_gelu)
            for n in range(IG - 2, IG):
                gelu(n, n)
            act.wait_ge(S["a_done"], 2 + IG * (g + 1))
            act.wait_ge(S["u_lo"], IG * (g + 1))
            spread = g + 1 < NG

            def v_high(s, i, e):
                u, v = e % VS, i * 8 + (IG * (NS * g + s) + e)
                act.wait_ge(S["v_mm"], v + 1)
                nc.scalar.copy(ah[u][:].rearrange("p (a n) -> p a n", a=1), gates[:, g % 2, bass.ds(i * 8 + e, 1), :])
                if e % 4 == 0:
                    act.wait_ge(S[f"vr_in{e // 4}"], (i + (IG // 8 * (NS * g + s) + 1)) * 64)
                nc.scalar.copy(vh[u][:].rearrange("p b (q d) -> p b q d", q=4),
                               vnat[e // 4][:, e % 4].rearrange("p q (b d) -> p b q d", b=4)).then_inc(S["v_hi"], 1)

            def late_spread(s, i, h):
                spread_out(i * 4 + (64 * (g + 1) + 16 * s + h - 2), i * (4 * NB) + NB * (16 * s + h - 2), bank[6 + h % 2], (g + 1) % 2)

            for s in range(NS):
                if s == 0:
                    for e in range(8):
                        v_high(s, 0, e)
                        if spread and e >= 5 and e % 2:
                            late_spread(s, 0, e // 2)
                with act.Fori(1 if s == 0 else 0, IG // 8) as i:
                    for e in range(8):
                        v_high(s, i, e)
                        if spread and e % 2:
                            late_spread(s, i, e // 2)
            if spread:
                for h in range(2):
                    late_spread(NS, 0, h)
        act.wait_ge(S["swept"], NG * NS)
        square_all(2, h1T, squares2, lambda c: None)
        root(("norm3",), 2, N)
        for i, (c, w) in enumerate(NTILES):
            for q in range(2):
                b = take(act, ("y", i, q))
                give(nc.scalar.copy(y_view(i, w, q), b[0:w, :].rearrange("n (b q d) -> n b q d", b=4, q=4)), ("y", i, q))

    def tail_pool(pool):

        def gate_rows(m, n0_, z):
            pool.wait_ge(S["hot_step"], m + 1)
            nc.gpsimd.tensor_tensor(hot1[z][:], hot1[z][:], five(gT, n0_, IG), ALU.mult).then_inc(S["ab_ready"], 1)

        for i in range(3):
            evacuated(pool, ("slots", i))
        pool.wait_ge(S["out_sent"], 32)
        nc.gpsimd.memset(zero[:].bitcast(F32), 0.0).then_inc(S["zero_set"], 1)
        with pool.Fori(0, N // NB // HS) as i:
            for z in range(HS):
                gate_rows(i * HS + z, i * (HS * NB) + NB * z, z)
        for g in range(NG):
            for s in range(NS):
                first = NS * g + s
                with pool.Fori(0, IG // 8) as i:
                    for e in range(8):
                        u = e % VS
                        pool.wait_ge(S["v_hi"], i * 8 + (IG * first + e + 1))
                        nc.gpsimd.tensor_tensor(al[u][:].rearrange("p (a n) -> p a n", a=1), gates[:, g % 2, bass.ds(i * 8 + e, 1), :],
                                                ah[u][:].bitcast(F32).rearrange("p (a n) -> p a n", a=1), ALU.subtract).then_inc(S["al_done"], 1)
                        if e % 2 and g + 1 < NG:
                            h = e // 2
                            gate_rows(i * 4 + (64 * (g + 1) + 16 * s + h), i * (4 * NB) + NB * (16 * s + h), h)

    def five(t_, n0_, w_):
        return t_[:, bass.ds(n0_, NB)].rearrange("p (n a) -> p n a", a=1).to_broadcast([P, NB, w_])

    def tail_vector(dve, link, mean, loop_copy):
        for q in range(SB):
            evacuated(dve, ("sO", q))
        dve.sem_inc(S["u_turned"], 2)
        dve.sem_inc(S["a_done"], 2)
        dve.sem_inc(S["v_lo"], 8)
        with dve.Fori(0, 4) as i:
            for c in range(4):
                dve.wait_ge(S["proj_mm"], i * 4 + (14 * 4 + 5 + c))
                dst = xT[:, bass.ds(i * 4 + c, 1), META:T]
                nc.vector.tensor_tensor(dst, dst, bank[c][:, 0:N].rearrange("p (a n) -> p a n", a=1), ALU.add)\
                    .then_inc(S["proj_lo" if c < 2 else "proj_hi"], 1)
        dve.wait_ge(S["proj_lo"], 2 + 2 * 18)
        dve.wait_ge(S["proj_hi"], 2 + 2 * 18)
        mean(("norm2",), 1, N)
        for k in range(KC):
            nc.vector.scalar_tensor_tensor(x2[:, k, :], h1T[:, k, :], gcol[:, 16 + k:17 + k], rnorm[:, 0:N], ALU.mult, ALU.mult).then_inc(S["x2_done"], 1)
        dve.wait_ge(S["x2_done"], KC)
        for k in range(KC):
            dve.wait_ge(S["x2h_done"], k + 1)
            nc.vector.tensor_tensor(x2l[:, k, :], x2[:, k, :], x2h[:, k, :].bitcast(F32), ALU.subtract).then_inc(S["x2l_done"], 1)
        loop_copy(3, qqT)
        for i, (c, w) in enumerate(NTILES):
            scores, z = sc[i % 2][0:w], i % 2
            for k in range(2 * PH):
                if k % 4 == 0:
                    evacuated(dve, ("pS", i, k // 4))
                for r in range(2):
                    top = best[0:w, k, 8 * r:8 * r + 8]
                    link(nc.vector.max(top, scores[:, k, :]))
                    ins = nc.vector.max_index(besti[0:w, k, 8 * r:8 * r + 8], top, scores[:, k, :])
                    if r == 0:
                        link(nc.vector.match_replace(scores[:, k, :], top, scores[:, k, :], GONE))
            ins.then_inc(S["cand_done"], 1)
            dve.wait_ge(S["cand_done"], i + 1)
            side = lambda t_, n: t_[0:w].rearrange("p (h s) k -> p h s k", s=2)[:, :, n, :]
            rows4 = lambda t_: t_.rearrange("p h (k a) -> p h k a", a=1).to_broadcast([w, PH, PK, PK])
            cols4 = lambda t_: t_.rearrange("p h (a k) -> p h a k", a=1).to_broadcast([w, PH, PK, PK])
            cview = cand[0:w].rearrange("p h (k j) -> p h k j", k=PK)
            link(nc.vector.tensor_tensor(cview, rows4(side(best, 0)), cols4(side(best, 1)), ALU.add))
            link(nc.vector.tensor_copy(bestf[0:w], besti[0:w]))
            for h in range(PH):
                for r in range(2):
                    top = sums[0:w, h, 8 * r:8 * r + 8]
                    link(nc.vector.max(top, cand[0:w, h, :]))
                    link(nc.vector.max_index(pair[0:w, h, 8 * r:8 * r + 8], top, cand[0:w, h, :]))
                    if r == 0:
                        link(nc.vector.match_replace(cand[0:w, h, :], top, cand[0:w, h, :], GONE))
            if i >= 2:
                take(dve, ("slots", i - 2))
            nc.vector.tensor_tensor(gate[z][0:w], sums[0:w], sums[0:w, :, 0:1].to_broadcast([w, PH, PK]), ALU.subtract).then_inc(S["best_done"], 1)
            link(nc.vector.tensor_scalar(place[0:w, 0], pair[0:w], 4, None, ALU.logical_shift_right))
            link(nc.vector.tensor_scalar(place[0:w, 1], pair[0:w], 15, None, ALU.bitwise_and))
            link(nc.vector.tensor_copy(placef[0:w], place[0:w]))
            for n in range(2):
                link(nc.vector.tensor_tensor(equal[0:w], rows4(placef[0:w, n]), cols4(iota[0:w, 0:PK].rearrange("p (h k) -> p h k", h=1).to_broadcast([w, PH, PK])), ALU.is_equal))
                link(nc.vector.tensor_tensor(equal[0:w], equal[0:w], cols4(side(bestf, n)), ALU.mult))
                link(nc.vector.tensor_reduce(slot[z][0:w, n, :].rearrange("p (h k) -> p h k", h=PH), equal[0:w], AX_X, ALU.add))
            dve.wait_ge(S["gate_exp"], i + 1)
            link(nc.vector.tensor_reduce(gsum[0:w, 0:PH], gate[z][0:w], AX_X, ALU.add))
            link(nc.vector.reciprocal(gsum[0:w, PH:2 * PH], gsum[0:w, 0:PH]))
            nc.vector.tensor_tensor(slot[z][0:w, 2, :].rearrange("p (h k) -> p h k", h=PH), gate[z][0:w],
                                    gsum[0:w, PH:2 * PH].rearrange("p (h a) -> p h a", a=1).to_broadcast([w, PH, PK]), ALU.mult).then_inc(S["slots_done"], 1)

        for i in range(3):
            evacuated(dve, ("slots", i))
        def hot(m, n0_, g, z):
            dve.wait_ge(S["g_mm"], m + 1)
            index = lambda c_, w_: iota[:, c_:c_ + w_].rearrange("p (a w) -> p a w", a=1).to_broadcast([P, NB, w_])
            nc.vector.tensor_tensor(hot2[z][:], index(0, P), five(i2T, n0_, P), ALU.is_equal)
            nc.vector.tensor_tensor(hot1[z][:], index(IG * g, IG), five(i1T, n0_, IG), ALU.is_equal).then_inc(S["hot_step"], 1)

        with dve.Fori(0, N // NB // HS) as i:
            for z in range(HS):
                hot(i * HS + z, i * (HS * NB) + NB * z, 0, z)

        for g in range(NG):
            dve.wait_ge(S["g_mm"], HS + 64 * (g + 1))
            if g:
                dve.wait_ge(S["v_mm"], VS + 128 * g)
            dve.wait_ge(S["g_evac"], HS + 64 * (g + 1))

            def turn(n, r_, loads):
                dve.wait_ge(S[f"u_in{r_ % 2}"], loads * 64)
                if r_ >= 2:
                    dve.wait_ge(S["act_mm"], n + IG * g)
                nc.vector.transpose(ut[r_ % 3][:].rearrange("p b (g e) -> p g b e", g=4),
                                    unat[r_ % 2][:].rearrange("p g (b d) -> p g b d", d=32)).then_inc(S["u_turned"], 1)

            def gated_act(n, r_):
                dve.wait_ge(S["gelu_done"], n + (IG * g + 1))
                dst = gates[:, g % 2, bass.ds(n, 1), :]
                nc.vector.tensor_tensor(dst, bank[4 + r_ % 2][:, 0:N].rearrange("p (a n) -> p a n", a=1), dst, ALU.mult).then_inc(S["a_done"], 1)

            def low_turn_gate(n, r_, pair):
                dve.wait_ge(S["u_hi"], n + (IG * g + 1))
                nc.vector.tensor_tensor(ul[r_ % 3][:], ut[r_ % 3][:], uh[r_ % 2][:].bitcast(F32), ALU.subtract).then_inc(S["u_lo"], 1)
                if r_ + 2 < IG:
                    turn(n + 2, r_ + 2, pair + (IG // 2 * g + 2))
                if r_ >= 1:
                    gated_act(n - 1, r_ - 1)

            for n in range(2):
                turn(n, n, IG // 2 * g + 1)
            tiles(dve, low_turn_gate)
            gated_act(IG - 1, IG - 1)
            dve.wait_ge(S["a_done"], 2 + IG * (g + 1))
            for s in range(NS):
                first = NS * g + s
                with dve.Fori(0, IG // 8) as i:
                    for e in range(8):
                        u, v = e % VS, i * 8 + (IG * first + e)
                        dve.wait_ge(S["v_hi"], v + 1)
                        nc.vector.tensor_tensor(vl[u][:].rearrange("p b (q d) -> p b q d", q=4),
                                                vnat[e // 4][:, e % 4].rearrange("p q (b d) -> p b q d", b=4),
                                                vh[u][:].bitcast(F32).rearrange("p b (q d) -> p b q d", q=4), ALU.subtract).then_inc(S["v_lo"], 1)
                        if e % 2 and g + 1 < NG:
                            h = e // 2
                            hot(i * 4 + (64 * (g + 1) + 16 * s + h), i * (4 * NB) + NB * (16 * s + h), g + 1, h)
                dve.wait_ge(S["sweep_mm"], first + 1)
                for d in range(4):
                    ins = nc.vector.tensor_tensor(h1T[:, 4 * s + d, :], h1T[:, 4 * s + d, :], bank[d][:, 0:N], ALU.add)
                ins.then_inc(S["swept"], 1)
        dve.wait_ge(S["swept"], NG * NS)
        mean(("norm3",), 2, N)
        for k in range(KC):
            nc.vector.scalar_tensor_tensor(yT[:, k, :], h1T[:, k, :], gcol[:, 32 + k:33 + k], rnorm[:, 0:N], ALU.mult, ALU.mult).then_inc(S["yT_done"], 1)
        for i, (c, w) in enumerate(NTILES):
            for q in range(2, 4):
                b = take(dve, ("y", i, q))
                give(nc.vector.tensor_copy(y_view(i, w, q), b[0:w, :].rearrange("n (b q d) -> n b q d", b=4, q=4)), ("y", i, q))

    with ctx:
        NC0 = 3 * P
        c0 = at("c0", 0, [P, NC0])
        ident, ones, iota = c0[:, 0:P], c0[:, P:2 * P], c0[:, 2 * P:3 * P]
        gcol = at("gcol", 1536, [P, 56])
        i1T = at("i1T", 2048, [P, N])
        i2T = at("i2T", 3328, [P, N])
        gT = at("gT", 4608, [P, N])
        rnorm = at("rnorm", 5888, [P, T])
        small = 7232
        xT = at("xT", 8192, [P, KC, T])
        h1T = xT[:, :, META:T]
        PR = 29696
        CH = T * 4
        projT = at("projT", PR, [P, NJ, T])
        xnat = at("xnat", PR, [P, 3, D])
        xperm = at("xperm", PR + 24576, [P, 3, D])
        wperm = [at(f"wperm{s}", PR + s * 16384, [P, KC, LD]) for s in range(2)]
        WR = PR + NJ * CH
        wring = [at(f"wring{s}", WR + s * 16384, [P, KC, LD]) for s in range(2)]
        xnT = at("xnT", WR + 33024, [P, KC, T])
        mixT = at("mixT", WR + 33024, [P, KC, N])
        NR = WR + 33024 + KC * CH
        mv_nat = at("mv_nat", NR, [P, 4, MH, DV + 1])
        av_nat = at("av_nat", NR + 16448, [P, 4, AH * DH])
        mk_nat = at("mk_nat", NR + 32832, [P, 4, MH * DK])
        squares = [at(f"squares{s}", NR + s * CH, [P, T]) for s in range(2)]
        gate_w = at("gate_w", NR, [P, KC, 8])
        idx_w = at("idx_w", 2048, [P, KC, ID + IH])
        grow = at("grow", NR + 2 * CH + 5632, [56, P])
        xnh = at("xnh", NR + 512, [P, KC, T], FR)
        xnl = at("xnl", WR + 33024, [P, KC, T], FR)
        wh = {n: [at(f"wh{n}_{s}", o_ + 8192 * s, [P, KC, P], FR) for s in range(2)]
              for n, o_ in ((0, NR + 22016), (3, WR + 33024 + 20480 + 24576))}
        wh[1] = wh[0]
        wl = [at(f"wl{s}", WR + s * 16384, [P, KC, LD], FR) for s in range(2)]
        CS = NR + 41024
        c1 = at("c1", CS, [P, const_at["bucket_hot"][0] - NC0])

        def const(name):
            c, shape = const_at[name]
            return c1[0:shape[0], c - NC0:c - NC0 + shape[1]]

        C0 = [at(f"C0_{s}", WR + s * 8224, [P, SB, DV + 1]) for s in range(2)]
        rows = WR + 16448
        lf = at("lf", rows, [MH, T])
        tmp = at("tmp", rows + CH, [MH, T])
        bcum = at("bcum", rows + 2 * CH, [MH, T])
        mrow = at("mrow", rows + 3 * CH, [MH, T])
        li = at("li", rows + 4 * CH, [MH, T])
        rrow = at("rrow", rows + 5 * CH, [MH, T])
        crow = at("crow", rows + 6 * CH, [MH, T])
        wrow = at("wrow", rows + 7 * CH, [MH, T])
        erow = at("erow", rows + 8 * CH, [MH, T])
        iwT = at("iwT", rows + 9 * CH, [IH, T])
        ikT = at("ikT", rows + 10 * CH, [P, T])
        cc = rows + 11 * CH
        ccol = at("ccol", cc, [P, 4, MH])
        ecol = at("ecol", cc + 64, [P, 3, MH])
        wcol = at("wcol", cc + 112, [P, 2, IH])
        n0 = at("n0", cc + 240, [P, SB, MH])
        abc = at("abc", cc + 368, [P, SB])
        st = at("st", cc + 400, [P, 8])
        bi = at("bi", small, [MH, 1])
        bf = at("bf", small + 4, [MH, 1])
        m0 = at("m0", small + 8, [MH, SB])
        pages = at("pages", small + 40, [1, SB * 2], I32)
        nrow = at("nrow", small + 104, [SB * MH, P])
        relb = at("relb", small + 616, [BUCKETS, AH])
        npr = at("npr", small + 648, [P, MH])
        nsa = at("nsa", small + 664, [P, SB * MH])
        nout = at("nout", WR + 33024 + 20480, [SB * MH, P])
        ML = PR + J_MV * CH
        decay = at("decay", ML, [P, 3, SEQ])
        gated = at("gated", ML + 3072, [P, 3, SEQ])
        hnorm = [at(f"hnorm{s}", ML + 6144 + 1024 * s, [P, DV]) for s in range(2)]
        kw = at("kw", ML + 8192, [P, 3, DK])
        cout = at("cout", ML + 9728, [P, DV])
        AV = PR + J_AV * CH
        qz = at("qz", AV, [P, SB * (TS + ST)])
        kwz = at("kwz", AV + 2304, [TS, SB, DK])
        MX = WR + 33024
        natk = [at(f"natk{s}", MX + s * 2048, [P, 512]) for s in range(2)]
        bhot = at("bhot", MX + 4096, [BUCKETS, RW])
        brow = at("brow", MX + 6208, [AH, RW])
        nki = at("nki", MX + 8320, [P, 4, ID])
        bt = at("bt", WR, [P, AH, BTW])
        bt_raw = at("bt_raw", NR, [P, AH, BTW])
        bs_raw = at("bs_raw", NR + 12800, [AH * ST, KS])
        score = at("score", AV, [P, TP])
        keep = at("keep", AV + 1088, [P, TP])
        top8 = at("top8", AV + 2176, [P, 8])
        relu = [at(f"relu{s}", AV + 2208 + s * 1088, [P, TP]) for s in range(3)]
        logit = [at(f"logit{s}", AV + 5472 + s * 1088, [P, TP]) for s in range(2)]
        probT = [at(f"probT{s}", AV + 7648 + s * 1536, [P, 3, P]) for s in range(2)]
        SI = PR + 16384
        iqz = at("iqz", SI, [P, SB, P])
        kin = [at(f"kin{s}", SI + 4096 + s * 1024, [P, 2, P]) for s in range(2)]
        kiT = [at(f"kiT{s}", SI + 6144 + s * 1056, [P, KS]) for s in range(2)]
        reluS = at("reluS", NR, [P, SB, KS])
        wz = at("wz", SI + 10368, [P, SB * (TS + ST)])
        kpage = [at(f"kpage{s}", NR + s * 8192, [P, 2, AH * DH]) for s in range(2)]
        vpage = [at(f"vpage{s}", PR + s * 8192, [P, 2, AH * DH]) for s in range(2)]
        vnew = [at(f"vnew{s}", NR + 32832 + s * 4096, [ST, AH * DH]) for s in range(2)]
        kT = at("kT", WR + 12800, [P, AH, PAST])
        qpad = at("qpad", AV, [P, SB, AH * (TS + ST)])
        SW = NR + 16448
        scoreS = at("scoreS", SW, [TS, KS])
        keepS = at("keepS", SW + 1056, [TS, KS])
        biasS = at("biasS", rows + 4 * CH, [AH * ST, KS])
        top8S = at("top8S", SW + 3168, [TS, 8])
        logitS = [at(f"logitS{s}", SW + 3200 + s * 1056, [AH * ST, KS]) for s in range(2)]
        probS = [at(f"probS{s}", SW + 5312 + s * 768, [P, 3, AH * ST]) for s in range(2)]
        stS = at("stS", SW + 6848, [AH * ST, 4])

        X2 = 29696
        x2h = at("x2h", X2, [P, KC, N], FR)
        x2l = at("x2l", X2 + 20480, [P, KC, N], FR)
        TA = X2 + 40960
        x2 = at("x2", TA, [P, KC, N])
        squares2 = [at(f"squares2_{n}", TA + 20480 + 1280 * n, [P, N]) for n in range(2)]
        equal = at("equal", TA + 23040, [P, PH, PK, PK])
        qqT = at("qqT", WR + 33024, [P, KC, N])
        KN = WR + 33024 + 20480
        knat = [at(f"knat{n}", KN + 8192 * n, [P, PH, P]) for n in range(2)]
        kT12 = at("kT12", KN + 16384, [P, 2 * PH, P])
        sc = [at(f"sc{n}", KN + 24576 + 8192 * n, [P, 2 * PH, NK]) for n in range(2)]
        cand = at("cand", KN + 40960, [P, PH, PK * PK])
        best = at("best", KN + 49152, [P, 2 * PH, PK])
        besti = at("besti", KN + 50176, [P, 2 * PH, PK], U32)
        bestf = at("bestf", KN + 51200, [P, 2 * PH, PK])
        place = at("place", TA + 31232, [P, 2, PH, PK], U32)
        placef = at("placef", KN + 52224, [P, 2, PH, PK])
        gsum = at("gsum", KN + 53248, [P, 2 * PH])
        pair = at("pair", KN + 53312, [P, PH, PK], U32)
        sums = at("sums", TA + 32256, [P, PH, PK])
        gate = [at(f"gate{n}", TA + 32768 + 512 * n, [P, PH, PK]) for n in range(2)]
        slot = [at(f"slot{n}", TA + 1536 * n, [P, 3, PH * PK]) for n in range(2)]
        gates = at("gates", TA, [P, 2, IG, N])
        UA = TA + 8 * IG * N
        unat = [at(f"unat{n}", UA + 8192 * n, [P, 4, 512]) for n in range(2)]
        vnat = [at(f"vnat{n}", UA + 8192 * n, [P, 4, 4, P]) for n in range(2)]
        ul = [at(f"ul{n}", UA + 16384 + 8192 * n, [P, KC, P], FR) for n in range(3)]
        ut = [at(f"ut{n}", UA + 16384 + 8192 * n, [P, KC, P]) for n in range(3)]
        uh = [at(f"uh{n}", UA + 40960 + 8192 * n, [P, KC, P], FR) for n in range(2)]
        vh = [at(f"vh{n}", UA + 16384 + 2048 * n, [P, 4, P], FR) for n in range(VS)]
        vl = [at(f"vl{n}", UA + 24576 + 2048 * n, [P, 4, P], FR) for n in range(VS)]
        ah = [at(f"ah{n}", UA + 32768 + 1280 * n, [P, N], FR) for n in range(VS)]
        al = [at(f"al{n}", UA + 37888 + 1280 * n, [P, N], FR) for n in range(VS)]
        hot1 = [at(f"hot1_{n}", UA + 43008 + 640 * n, [P, NB, IG]) for n in range(HS)]
        hot2 = [at(f"hot2_{n}", UA + 45568 + 2560 * n, [P, NB, P]) for n in range(HS)]
        zero = at("zero", small, [P, P], FR)
        yT = at("yT", TA + 40960, [P, KC, N])
        ynat = [at(f"ynat{n}", UA + 8192 * n, [P, D]) for n in range(3)]

        bank = [ctx.enter_context(nc.psum_tensor(f"bank{i}", [P, 512], F32)) for i in range(8)]
        rb_dram = nc.dram_tensor("rb_dram", (AH, RW), F32).ap()

        bank_free = [sem(f"bank_free{i}") for i in range(8)]
        mm_ready = sem("mm_ready")
        S = {n: sem(n) for n in (
            "const_in", "ki_sent", "v_sent", "m_sent", "nsa_done", "attn_done", "small_in", "x_in", "x_perm",
            "wp_done", "gatew_in", "bhot_in", "bt_in", "act_step", "vec_step", "square", "square_used",
            "rnorm_sqrt", "rnorm_done", "xn_done", "xnh_done", "xnl_done", "w_hi", "w_lo", "w_in0", "w_in1",
            "proj_mm", "proj_lo", "proj_hi", "gates", "gates_ln", "rows_done", "rows_exp", "ones_set",
            "decay_done", "kw_done", "hn", "ssq", "rms", "cout_sent", "c_in0", "c_in1", "c_sent0", "c_sent1",
            "qz_zero", "kwz_done", "natk_sent0", "natk_sent1", "out_sent", "row_sent", "relu_used", "logit_done",
            "exp_done", "prob_done", "iqz_zero", "iqz_done", "kin_in0", "kin_in1", "wz_done", "keepS_done",
            "qpad_zero", "qpad_done", "k_in0", "k_in1", "v_in0", "v_in1", "logitS_done", "expS_done", "probS_done",
            "x2_done", "x2h_done", "x2l_done", "slots_done", "cand_done", "best_done", "gate_exp", "zero_set",
            "hot_step", "al_done", "ab_ready", "g_mm", "g_evac", "u_in0", "u_in1", "vr_in0", "vr_in1", "u_turned",
            "u_hi", "u_lo", "act_mm", "gelu_done", "a_done", "v_hi", "v_lo", "v_mm", "swept", "sweep_mm",
            "yT_done", "knat_in",
        )}

        def in_chunks(rows_):
            return rows_.rearrange("n (q b d) -> n b q d", q=4, d=32)

        def chunks(rows_):
            return rows_.rearrange("n (b q d) -> n b q d", q=4, d=32)

        def take(eng, key):
            eng.wait_ge(mm_ready, JOB[key] + 1)
            return bank[JOB[key] % 8]

        def give(ins, key):
            return ins.then_inc(bank_free[JOB[key] % 8], 1)

        def evacuated(eng, key):
            eng.wait_ge(bank_free[JOB[key] % 8], JOB[key] // 8 + 1)

        def banks_idle(eng, key, which=range(8)):
            for b in which:
                n = (JOB[key] - b) // 8 + 1
                if n > 0:
                    eng.wait_ge(bank_free[b], n)

        w_parts = [
            (a["w_in"][0], C_MQ, 6), (a["w_in"][0], C_AQ, 8), (a["w_out"][0], 0, 4), (a["peer_wq"][0], 0, 4)]
        w_first = [0, 6, 14, 18]
        split_from = {0: 0, 1: 24, 3: 56}
        scale_k = float(DK) ** -0.5
        scale_a = float(DH) ** -0.5
        scale_i = float(ID) ** -0.5 * float(IH) ** -0.5
        block = ctx.enter_context(nc.Block())
        outs_sent = [0]

        @block.sync
        def _(sp):
            def out(dst, src):
                outs_sent[0] += 1
                sp.dma_start(dst, src).then_inc(S["out_sent"], 16)

            def load_weights(n):
                w, col, iters = w_parts[n]
                with sp.Fori(0, iters) as i:
                    for s in range(2):
                        sp.wait_ge(S["proj_mm"], (i + w_first[n]) * 4 + 2 * (s + 1))
                        for q in range(4):
                            if n == 2:
                                src = w.rearrange("(k p) (q c) -> q p k c", p=P, q=4)[q, :, :, bass.ds(i * P + 64 * s, 64)]
                                dst = wring[s][:, :, 64 * q:64 * q + 64]
                            else:
                                src = w.rearrange("(q b d) n -> q d b n", q=4, d=32)[q, :, :, bass.ds(i * (2 * LD) + (col + LD * s), LD)]
                                dst = wring[s][32 * q:32 * q + 32]
                            sp.dma_start(dst, src).then_inc(S[f"w_in{s}"], 16)

            sp.dma_start(c0[:], consts[:, 0:NC0]).then_inc(S["const_in"], 16)
            xp, xs, mt = a["x_prompt"][0], a["x_sample"].rearrange("b t d -> (b t) d"), a["meta_tokens"]
            sp.dma_start(xnat[0:META, 0, :], mt).then_inc(S["x_in"], 16)
            sp.dma_start(xnat[META:P, 0, :], xp[0:P - META]).then_inc(S["x_in"], 16)
            sp.dma_start(xnat[:, 1, :], xp[P - META:2 * P - META]).then_inc(S["x_in"], 16)
            sp.dma_start(xnat[0:META, 2, :], xp[2 * P - META:SEQ]).then_inc(S["x_in"], 16)
            sp.dma_start(xnat[META:META + TS, 2, :], xs).then_inc(S["x_in"], 16)
            for r, g in ((0, a["norm1_g"][0]), (16, a["norm2_g"][0]), (32, a["final_norm_g"])):
                sp.dma_start(grow[r:r + KC, :].rearrange("b (q d) -> b q d", q=4), g.rearrange("(q b d) -> b q d", q=4, d=32)).then_inc(S["small_in"], 16)
            sp.dma_start(grow[48:56, :], a["mh_norm_g"][0].rearrange("(k p) -> k p", p=P)).then_inc(S["small_in"], 16)
            sp.dma_start(c1[:], consts[:, NC0:NC0 + c1.shape[1]]).then_inc(S["small_in"], 16)
            sp.dma_start(bi[:], a["b_i"].rearrange("a h -> h a")).then_inc(S["small_in"], 16)
            sp.dma_start(bf[:], a["b_f"].rearrange("a h -> h a")).then_inc(S["small_in"], 16)
            sp.dma_start(m0[:], a["state_m"][0].rearrange("b h -> h b"), allow_slow_non_contiguous=True).then_inc(S["small_in"], 16)
            sp.dma_start(pages[:], a["page_table"].rearrange("b g -> (b g)").rearrange("(a n) -> a n", a=1)).then_inc(S["small_in"], 16)
            sp.dma_start(nrow[:], a["state_n"][0].rearrange("b h d -> (b h) d")).then_inc(S["small_in"], 16)
            sp.dma_start(relb[:], a["rel_bias"]).then_inc(S["small_in"], 16)
            load_weights(0)
            w = a["w_in"][0].rearrange("(q b d) n -> q d b n", q=4, d=32)
            sp.wait_ge(S["xn_done"], KC)
            for q in range(4):
                sp.dma_start(gate_w[32 * q:32 * q + 32], w[q, :, :, C_IG:C_IG + 8]).then_inc(S["gatew_in"], 16)
                sp.dma_start(idx_w[32 * q:32 * q + 32], w[q, :, :, C_IK:C_IK + ID + IH]).then_inc(S["gatew_in"], 16)
            load_weights(1)

            evacuated(sp, ("iw",))
            cb = const_at["bucket_hot"][0]
            sp.dma_start(bhot[:], consts[0:BUCKETS, cb:cb + RW]).then_inc(S["bhot_in"], 16)

            def rows_out(name, i, c=None):
                c0_, w_ = NAT[i]
                if i < 3:
                    dst = o[f"{name}_prompt"][0, 0]
                    dst = dst.rearrange("t h d -> t (h d)") if name != "kidx" else dst
                    dst = dst[c0_:c0_ + w_]
                else:
                    dst = o[f"{name}_sample"][0].rearrange("b t h d -> (b t) (h d)") if name != "kidx" \
                        else o[f"{name}_sample"][0].rearrange("b t d -> (b t) d")
                if c is not None:
                    dst = dst[:, c:c + 512]
                return dst

            evacuated(sp, ("natki",))
            for i, (_, w_) in enumerate(NAT):
                sp.dma_start(rows_out("kidx", i), nki[0:w_, i, :]).then_inc(S["ki_sent"], 16)
            for i, (_, w_) in enumerate(NAT):
                evacuated(sp, ("nat", i, 3))
                evacuated(sp, ("nat", i, 2))
                sp.dma_start(rows_out("v", i), av_nat[0:w_, i, :]).then_inc(S["v_sent"], 16)
                for q in (4, 5):
                    evacuated(sp, ("nat", i, q))
                    sp.dma_start(rows_out("k", i, 512 * (q - 4)), natk[q % 2][0:w_, :])\
                        .then_inc(S[f"natk_sent{q % 2}"], 16)
            for n in range(2):
                evacuated(sp, ("bias", n))
            sp.dma_start(rb_dram, brow[:]).then_inc(S["row_sent"], 16)
            sp.wait_ge(S["row_sent"], 16)

            def load_C(h):
                s = h % 2
                sp.dma_start(C0[s][:, :, 0:DV], a["state_C"][0][:, h].rearrange("b k v -> k b v")).then_inc(S[f"c_in{s}"], 16)

            load_C(0)
            load_C(1)
            for h in range(MH):
                evacuated(sp, ("mC", h))
                sp.dma_start(o["C_prompt"][0, 0, h], cout[:]).then_inc(S["cout_sent"], 16)
            for h in range(MH):
                s = h % 2
                evacuated(sp, ("sC", h, SB - 1))
                sp.dma_start(o["C_sample"][0][:, h].rearrange("b k v -> k b v"), C0[s][:, :, 0:DV]).then_inc(S[f"c_sent{s}"], 16)
                if h + 2 < MH:
                    sp.wait_ge(S[f"c_sent{s}"], 16 * (h // 2 + 1))
                    sp.wait_ge(S["nsa_done"], h + 1)
                    load_C(h + 2)
            sp.dma_start(o["m_prompt"][0].rearrange("a h -> h a"), mrow[:, TP - 1:TP], allow_slow_non_contiguous=True).then_inc(S["m_sent"], 16)
            sp.dma_start(o["m_sample"][0].rearrange("b h -> h b"),
                         mrow[:, TP:T].rearrange("h (b t) -> h b t", t=ST)[:, :, ST - 1], allow_slow_non_contiguous=True).then_inc(S["m_sent"], 16)
            evacuated(sp, ("nout",))
            out(o["n_prompt"][0, 0], nrow[0:MH, :])
            out(o["n_sample"][0].rearrange("b h d -> (b h) d"), nout[:])
            for s in range(2):
                sp.wait_ge(S[f"c_sent{s}"], 32)
                sp.wait_ge(S[f"natk_sent{s}"], 64)
            sp.wait_ge(S["cout_sent"], 64)
            src = bass.AP(tensor=rb_dram.tensor, offset=rb_dram.offset, ap=[[1, P], [RW, AH], [1, BTW]])
            sp.dma_start(bt_raw[:], src).then_inc(S["bt_in"], 16)
            for h in range(AH):
                src = bass.AP(tensor=rb_dram.tensor, offset=rb_dram.offset + RW * h + 8, ap=[[1, ST], [1, KS]])
                sp.dma_start(bs_raw[ST * h:ST * h + ST], src).then_inc(S["bt_in"], 16)
            page = [sp.value_load(pages[0:1, n:n + 1], min_val=0, max_val=a["cache_k"].shape[1] - 1) for n in range(2 * SB)]
            for b in range(SB):
                s = b % 2
                if b >= 2:
                    evacuated(sp, ("cki", b - 2))
                for g in range(2):
                    for c in range(2):
                        sp.dma_start(kin[s][:, g, c * ID:(c + 1) * ID], a["cache_kidx"][0, page[2 * b + g]])\
                            .then_inc(S[f"kin_in{s}"], 16)
            evacuated(sp, ("sScore",))
            for b in range(SB):
                s = b % 2
                if b >= 2:
                    evacuated(sp, ("sK", b - 2, 3))
                    evacuated(sp, ("sO", b - 2))
                for g in range(2):
                    sp.dma_start(kpage[s][:, g, :], a["cache_k"][0, page[2 * b + g]].rearrange("t h d -> t (h d)")).then_inc(S[f"k_in{s}"], 16)
                    sp.dma_start(vpage[s][:, g, :], a["cache_v"][0, page[2 * b + g]].rearrange("t h d -> t (h d)")).then_inc(S[f"v_in{s}"], 16)
                sp.dma_start(vnew[s][:], av_nat[ST * b:ST * b + ST, 3, :]).then_inc(S[f"v_in{s}"], 16)
            tail_sync(sp, out, load_weights)
            sp.wait_ge(S["out_sent"], 16 * outs_sent[0])

        @block.tensor
        def _(pe):
            def open_bank(key):
                if JOB[key] >= 8:
                    pe.wait_ge(bank_free[JOB[key] % 8], JOB[key] // 8)
                return bank[JOB[key] % 8]

            def close(mm):
                mm.then_inc(mm_ready, 1)

            def flip(out_, in_, rows):
                return pe.transpose(out_, in_, ident[0:rows, 0:rows])

            def norm_sum(key, turn, width, squares_):
                b = open_bank(key)
                for c in range(KC):
                    pe.wait_ge(S["square"], KC * turn + c + 1)
                    mm = pe.matmul(b[:, 0:width], ones, squares_[c % 2][:, 0:width], start=(c == 0), stop=(c == KC - 1))
                    if c < KC - 1:
                        mm.then_inc(S["square_used"], 1)
                close(mm)

            def weight_loop(n, rhs):
                first, iters, width = w_first[n], w_parts[n][2], N if n > 1 else T
                with pe.Fori(0, iters) as i:
                    for s in range(2):
                        if n == 2:
                            pe.wait_ge(S["wp_done"], i * 2 + (s + 1))
                        for c in range(2):
                            dst_ = bank[2 * s + c][:, 0:width]
                            if n != 2:
                                pe.wait_ge(S["w_lo"], i * 4 + (split_from[n] + 2 * s + c + 1))
                            pe.wait_ge(S["proj_lo" if s == 0 else "proj_hi"], (i + first) * 2 + (c + 1))
                            for k in range(KC):
                                if n == 2:
                                    mm = pe.matmul(dst_, wperm[s][:, k, c * P:(c + 1) * P], rhs[:, k, :], start=(k == 0), stop=(k == KC - 1))
                                    continue
                                pe.matmul(dst_, wh[n][c][:, k, :], rhs[0][:, k, :], start=(k == 0), stop=False)
                                pe.matmul(dst_, wh[n][c][:, k, :], rhs[1][:, k, :], start=False, stop=False)
                                mm = pe.matmul(dst_, wl[s][:, k, c * P:(c + 1) * P], rhs[0][:, k, :], start=False, stop=(k == KC - 1))
                            mm.then_inc(S["proj_mm"], 1)

            def loop_read(n):
                done = 2 + 2 * (w_first[n] + w_parts[n][2])
                pe.wait_ge(S["proj_lo"], done)
                pe.wait_ge(S["proj_hi"], done)

            pe.sem_inc(S["proj_mm"], 4)
            pe.wait_ge(S["const_in"], 16)
            for i, (_, w) in enumerate(XTILES):
                pe.wait_ge(S["x_perm"], i + 1)
                for q in range(4):
                    b = open_bank(("x", i, q))
                    for c in range(4):
                        mm = flip(b[:, c * w:(c + 1) * w], xperm[0:w, i, (4 * q + c) * P:(4 * q + c + 1) * P], w)
                    close(mm)
            pe.wait_ge(S["small_in"], 16 * SMALL_LOADS)
            close(flip(open_bank(("gcols",))[:, 0:56], grow[:], 56))
            norm_sum(("norm1",), 0, T, squares)
            banks_idle(pe, ("norm1",), range(4))
            pe.wait_ge(S["xnl_done"], KC)
            weight_loop(0, (xnh, xnl))
            weight_loop(1, (xnh, xnl))
            loop_read(1)
            pe.wait_ge(S["gatew_in"], 128)
            for n in range(2):
                b = open_bank(("gate", n))
                for k in range(KC):
                    pe.matmul(b[0:MH, 0:T], gate_w[:, k, MH * n:MH * n + MH], xnh[:, k, :].bitcast(F32), start=(k == 0), stop=False)
                    mm = pe.matmul(b[0:MH, 0:T], gate_w[:, k, MH * n:MH * n + MH], xnl[:, k, :].bitcast(F32), start=False, stop=(k == KC - 1))
                close(mm)
            b = open_bank(("ik",))
            for e in range(2):
                for k in range(KC):
                    pe.matmul(b[ID * e:ID * e + ID, 0:T], idx_w[:, k, 0:ID], xnh[:, k, :].bitcast(F32), start=(k == 0), stop=False)
                    mm = pe.matmul(b[ID * e:ID * e + ID, 0:T], idx_w[:, k, 0:ID], xnl[:, k, :].bitcast(F32), start=False, stop=(k == KC - 1))
            close(mm)
            b = open_bank(("iw",))
            for k in range(KC):
                pe.matmul(b[0:IH, 0:T], idx_w[:, k, ID:ID + IH], xnh[:, k, :].bitcast(F32), start=(k == 0), stop=False)
                mm = pe.matmul(b[0:IH, 0:T], idx_w[:, k, ID:ID + IH], xnl[:, k, :].bitcast(F32), start=False, stop=(k == KC - 1))
            close(mm)
            b = open_bank(("natki",))
            evacuated(pe, ("ik",))
            for i, (c, w) in enumerate(NAT):
                mm = flip(b[0:w, ID * i:ID * i + ID], ikT[0:ID, c:c + w], ID)
            close(mm)
            for i, (c, w) in enumerate(NAT):
                for q, j in enumerate((J_MV, J_MV + 4, J_AV, J_AV + 4, J_AK, J_AK + 4, J_MK)):
                    b = open_bank(("nat", i, q))
                    for n in range(4):
                        mm = flip(b[0:w, n * P:(n + 1) * P], projT[:, j + n, c:c + w], P)
                    close(mm)
            b = open_bank(("cols",))
            pe.wait_ge(S["rows_done"], 1)
            pe.wait_ge(S["rows_exp"], 1)
            for j, (c, w) in enumerate(NAT):
                mm = flip(b[0:w, MH * j:MH * j + MH], crow[:, c:c + w], MH)
            for j, (c, w) in enumerate(NTILES):
                mm = flip(b[0:w, 16 + MH * j:16 + MH * j + MH], erow[:, META + c:META + c + w], MH)
            close(mm)
            b = open_bank(("wcol",))
            evacuated(pe, ("iw",))
            for i in range(2):
                mm = flip(b[:, IH * i:IH * i + IH], iwT[:, META + P * i:META + P * i + P], IH)
            close(mm)
            close(flip(open_bank(("n0",))[:, 0:SB * MH], nrow[:], SB * MH))
            pe.wait_ge(S["bhot_in"], 16)
            for n in range(2):
                b = open_bank(("bias", n))
                close(pe.matmul(b[0:AH, 0:RW // 2], relb[:], bhot[:, n * (RW // 2):(n + 1) * (RW // 2)], start=True, stop=True))

            for h in range(MH):
                sel = const("head_row")[:, h * P:(h + 1) * P]
                close(pe.matmul(open_bank(("mR", h))[:, 0:SEQ], sel, rrow[:, META:TP], start=True, stop=True))
                for j in range(3):
                    c, w = NAT[j]
                    b = open_bank(("mS", h, j))
                    close(pe.matmul(b[0:w, 0:SEQ], projT[:, J_MK + h, c:c + w], projT[:, J_MQ + h, META:TP], start=True, stop=True))
                for i in range(2):
                    b = open_bank(("mN", h, i))
                    for j in range(2 + i):
                        w = NAT[j][1]
                        evacuated(pe, ("mS", h, j))
                        mm = pe.matmul(b[:, 0:DV + 1], gated[0:w, j, P * i:P * i + P], mv_nat[0:w, j, h, :], start=(j == 0), stop=(j == 1 + i))
                    close(mm)
                b = open_bank(("mC", h))
                pe.wait_ge(S["kw_done"], h + 1)
                for j in range(3):
                    w = NAT[j][1]
                    mm = pe.matmul(b[:, 0:DV + 1], kw[0:w, j, :], mv_nat[0:w, j, h, :], start=(j == 0), stop=(j == 2))
                close(mm)
                for i in range(2):
                    b = open_bank(("mT", h, i))
                    pe.wait_ge(S["hn"], 2 * h + i + 1)
                    for c in range(2):
                        mm = flip(b[:, c * P:(c + 1) * P], hnorm[i][:, c * P:(c + 1) * P], P)
                    close(mm)
            for h in range(MH):
                s = h % 2
                sel = const("head_row")[:, h * P:(h + 1) * P]
                close(pe.matmul(open_bank(("sR", h))[:, 0:TS], sel, rrow[:, TP:T], start=True, stop=True))
                close(pe.matmul(open_bank(("sW", h))[:, 0:TS], sel, wrow[:, TP:T], start=True, stop=True))
                b = open_bank(("sS", h))
                close(pe.matmul(b[0:TS, 0:TS], projT[:, J_MK + h, TP:T], projT[:, J_MQ + h, TP:T], start=True, stop=True))
                b = open_bank(("sN", h))
                pe.wait_ge(S[f"c_in{s}"], 16 * (h // 2 + 1))
                evacuated(pe, ("sW", h))
                for q in range(SB):
                    pe.matmul(b[0:TS, 0:DV + 1], qz[:, q * TS:(q + 1) * TS], C0[s][:, q, :], start=(q == 0), stop=False)
                evacuated(pe, ("sS", h))
                close(pe.matmul(b[0:TS, 0:DV + 1], gated[0:TS, 0, 0:TS], mv_nat[0:TS, 3, h, :], start=False, stop=True))
                b = open_bank(("sT", h))
                pe.wait_ge(S["hn"], 2 * MH + h + 1)
                for c in range(2):
                    mm = flip(b[:, c * TS:(c + 1) * TS], hnorm[0][0:TS, c * P:(c + 1) * P], TS)
                close(mm)
                for q in range(SB):
                    b = open_bank(("sC", h, q))
                    pe.wait_ge(S["kwz_done"], h + 1)
                    close(pe.matmul(b[:, 0:DV + 1], kwz[:, q, :], mv_nat[0:TS, 3, h, :], start=True, stop=True))
            b = open_bank(("nout",))
            pe.wait_ge(S["nsa_done"], MH)
            flip(b[0:MH, 0:P], npr[:], P)
            close(flip(b[0:SB * MH, P:2 * P], nsa[:], P))

            pe.wait_ge(S["bt_in"], 16 * (1 + AH))
            for h in range(AH):
                close(pe.matmul(open_bank(("bt", h))[:, 0:BTW], const("flip"), bt_raw[:, h, :], start=True, stop=True))
            close(pe.matmul(open_bank(("bs",))[0:AH * ST, 0:KS], const("flip_t"), bs_raw[:], start=True, stop=True))
            for i in range(2):
                t0 = META + P * i
                for h in range(IH):
                    e = ID * (h % 2)
                    b = open_bank(("ix", i, h))
                    close(pe.matmul(b[:, 0:TP], projT[e:e + ID, J_IQ + h // 2, t0:t0 + P], ikT[e:e + ID, 0:TP], start=True, stop=True))
                for h in range(AH + 1):
                    if h < AH:
                        b = open_bank(("aL", i, h))
                        close(pe.matmul(b[:, 0:TP], projT[:, J_AQ + h, t0:t0 + P], projT[:, J_AK + h, 0:TP], start=True, stop=True))
                    if h >= 1:
                        k = i * AH + h - 1
                        b = open_bank(("aP", i, h - 1))
                        pe.wait_ge(S["prob_done"], k + 1)
                        for j in range(3):
                            c, w = NAT[j]
                            mm = flip(b[0:w, j * P:(j + 1) * P], logit[k % 2][:, c:c + w], P)
                        close(mm)
                        b = open_bank(("aO", i, h - 1))
                        evacuated(pe, ("aP", i, h - 1))
                        for j in range(3):
                            w = NAT[j][1]
                            mm = pe.matmul(b[:, 0:P], av_nat[0:w, j, DH * (h - 1):DH * h], probT[k % 2][0:w, j, :], start=(j == 0), stop=(j == 2))
                        close(mm)

            close(pe.matmul(open_bank(("wrep",))[:, 0:TS], const("spread_h"), iwT[:, TP:T], start=True, stop=True))
            for q in range(SB):
                b = open_bank(("cki", q))
                pe.wait_ge(S[f"kin_in{q % 2}"], 64 * (q // 2 + 1))
                for g in range(2):
                    mm = flip(b[:, g * P:(g + 1) * P], kin[q % 2][:, g, :], P)
                close(mm)
                b = open_bank(("sI", q))
                pe.wait_ge(S["iqz_done"], 1)
                evacuated(pe, ("cki", q))
                pe.matmul(b[:, 0:PAST], iqz[:, q, :], kiT[q % 2][:, 0:PAST], start=True, stop=True)
                close(pe.matmul(b[:, PAST:KS], iqz[:, q, :], ikT[:, TP + ST * q:TP + ST * (q + 1)], start=True, stop=True))
            b = open_bank(("sScore",))
            for q in range(SB):
                if q == 0:
                    pe.wait_ge(S["wz_done"], 1)
                evacuated(pe, ("sI", q))
                mm = pe.matmul(b[0:TS, 0:KS], wz[:, q * TS:(q + 1) * TS], reluS[:, q, :], start=(q == 0), stop=(q == SB - 1))
            close(mm)
            for q in range(SB):
                for n in range(4):
                    b = open_bank(("sK", q, n))
                    pe.wait_ge(S[f"k_in{q % 2}"], 32 * (q // 2 + 1))
                    for e in range(2):
                        h = 2 * n + e
                        for g in range(2):
                            mm = flip(b[:, (2 * e + g) * P:(2 * e + g + 1) * P], kpage[q % 2][:, g, h * DH:(h + 1) * DH], P)
                    close(mm)
                b = open_bank(("sL", q))
                pe.wait_ge(S["qpad_done"], 1)
                pick = const("pick_b")[:, q * AH * ST:(q + 1) * AH * ST]
                rows_ = b[0:AH * ST]
                for h in range(AH):
                    if h % 2 == 0:
                        evacuated(pe, ("sK", q, h // 2))
                    lhs = qpad[:, q, h * AH * ST:(h + 1) * AH * ST]
                    pe.matmul(rows_[:, 0:PAST], lhs, kT[:, h, :], start=(h == 0), stop=False, skip_group_check=True)
                    pe.matmul(rows_[:, PAST:KS], lhs, projT[:, J_AK + h, TP + ST * q:TP + ST * (q + 1)],
                              start=False, stop=False, skip_group_check=True)
                pe.wait_ge(S["keepS_done"], 1)
                close(pe.matmul(rows_[:, 0:KS], pick, keepS[:], start=False, stop=True, skip_group_check=True))
                b = open_bank(("sP", q))
                pe.wait_ge(S["probS_done"], q + 1)
                for j, (c, w) in enumerate(((0, P), (P, P), (PAST, ST))):
                    mm = flip(b[0:w, j * AH * ST:(j + 1) * AH * ST], logitS[q % 2][:, c:c + w], AH * ST)
                close(mm)
                b = open_bank(("sO", q))
                evacuated(pe, ("sP", q))
                pe.wait_ge(S[f"v_in{q % 2}"], 48 * (q // 2 + 1))
                for h in range(AH):
                    cols = slice(ST * h, ST * h + ST)
                    for g in range(2):
                        pe.matmul(b[:, cols], vpage[q % 2][:, g, h * DH:(h + 1) * DH], probS[q % 2][:, g, cols], start=(g == 0), stop=False)
                    mm = pe.matmul(b[:, cols], vnew[q % 2][:, h * DH:(h + 1) * DH], probS[q % 2][0:ST, 2, cols], start=False, stop=True)
                close(mm)
            tail_tensor(pe, open_bank, close, flip, norm_sum, weight_loop, loop_read)

        @block.scalar
        def _(act):
            steps = [0]

            def link(ins):
                steps[0] += 1
                ins.then_inc(S["act_step"], 1)
                act.wait_ge(S["act_step"], steps[0])

            def square_all(turn, src, squares_, ready):
                for c in range(KC):
                    ready(c)
                    if c >= 2:
                        act.wait_ge(S["square_used"], (KC - 1) * turn + c - 1)
                    nc.scalar.activation(squares_[c % 2][:, 0:src.shape[2]], src[:, c, :], ACT.Square).then_inc(S["square"], 1)

            def root(key, turn, width):
                evacuated(act, key)
                nc.scalar.activation(rnorm[:, 0:width], rnorm[:, 0:width], ACT.Sqrt).then_inc(S["rnorm_sqrt"], 1)

            def loop_copy(n, dst):
                first, iters, width = w_first[n], w_parts[n][2], dst.shape[2]
                def high(i, c):
                    if c % 2 == 0:
                        act.wait_ge(S[f"w_in{c // 2}"], (i + (first + 1)) * 64)
                    act.wait_ge(S["proj_mm"], (i + first) * 4 + (c + 3))
                    nc.scalar.copy(wh[n][c % 2][:], wring[c // 2][:, :, P * (c % 2):P * (c % 2) + P]).then_inc(S["w_hi"], 1)

                with act.Fori(0, iters) as i:
                    high(i, 0)
                    high(i, 1)
                    for c in range(2):
                        high(i, 2 + c)
                        act.wait_ge(S["proj_mm"], (i + first) * 4 + (5 + c))
                        nc.scalar.copy(dst[:, bass.ds(i * 4 + c, 1), :], bank[c][:, 0:width].rearrange("p (a t) -> p a t", a=1))\
                            .then_inc(S["proj_lo"], 1)

            act.sem_inc(S["proj_lo"], 2)
            act.wait_ge(S["x_in"], 80)
            for i, (_, w) in enumerate(XTILES):
                nc.scalar.copy(chunks(xperm[0:w, i, :]), in_chunks(xnat[0:w, i, :])).then_inc(S["x_perm"], 1)
            for i, (c, w) in enumerate(XTILES):
                for q in (1, 3):
                    b = take(act, ("x", i, q))
                    give(nc.scalar.copy(xT[:, 4 * q:4 * q + 4, c:c + w], b[:, 0:4 * w].rearrange("p (n w) -> p n w", n=4)), ("x", i, q))

            def x_ready(c):
                if c % 4 == 0:
                    for i in range(3):
                        evacuated(act, ("x", i, c // 4))

            square_all(0, xT, squares, x_ready)
            root(("norm1",), 0, T)
            for k in range(KC):
                act.wait_ge(S["xn_done"], k + 1)
                nc.scalar.copy(xnh[:, k, :], xnT[:, k, :]).then_inc(S["xnh_done"], 1)
            loop_copy(0, projT[:, 0:J_AQ, :])
            loop_copy(1, projT[:, J_AQ:NJ, :])
            b = take(act, ("ik",))
            give(nc.scalar.copy(ikT[:], b[:, 0:T]), ("ik",))
            b = take(act, ("iw",))
            give(nc.scalar.mul(iwT[:], b[0:IH, 0:T], scale_i), ("iw",))
            act.wait_ge(S["proj_hi"], 2 + 2 * 14)
            link(nc.scalar.activation(projT[:, J_MO:J_MO + 8, :], projT[:, J_MO:J_MO + 8, :], ACT.Sigmoid))
            act.wait_ge(S["gates"], 1)
            link(nc.scalar.activation(tmp[:], tmp[:], ACT.Exp, scale=-1.0))
            nc.scalar.activation(tmp[:], tmp[:], ACT.Ln, bias=1.0).then_inc(S["gates_ln"], 1)
            b = take(act, ("natki",))
            for i, (_, w) in enumerate(NAT):
                ins = nc.scalar.copy(nki[0:w, i, :], b[0:w, ID * i:ID * i + ID])
            give(ins, ("natki",))
            for i, (_, w) in enumerate(NAT):
                for q in (2, 3, 4, 5):
                    if q >= 4 and i:
                        act.wait_ge(S[f"natk_sent{q % 2}"], 16 * i)
                    b = take(act, ("nat", i, q))
                    dst = av_nat[0:w, i, (q - 2) * 512:(q - 1) * 512] if q < 4 else natk[q % 2][0:w, :]
                    give(nc.scalar.copy(dst, b[0:w, :]), ("nat", i, q))
            act.wait_ge(S["rows_done"], 1)
            nc.scalar.activation(erow[:], mrow[:], ACT.Exp, scale=-1.0)
            nc.scalar.activation(wrow[:, TP:T], wrow[:, TP:T], ACT.Exp).then_inc(S["rows_exp"], 1)
            for h in range(MH):
                evacuated(act, ("mR", h))
                nc.scalar.activation(decay[:, 0:2, :], decay[:, 0:2, :], ACT.Exp)
                nc.scalar.activation(decay[0:META, 2, :], decay[0:META, 2, :], ACT.Exp).then_inc(S["decay_done"], 1)
                for i in range(2):
                    act.wait_ge(S["ssq"], 2 * h + i + 1)
                    nc.scalar.activation(st[:, 4 + i:5 + i], st[:, 4 + i:5 + i], ACT.Sqrt).then_inc(S["rms"], 1)
            for h in range(MH):
                evacuated(act, ("sR", h))
                nc.scalar.activation(decay[0:TS, 0, 0:TS], decay[0:TS, 0, 0:TS], ACT.Exp).then_inc(S["decay_done"], 1)
                act.wait_ge(S["ssq"], 2 * MH + h + 1)
                nc.scalar.activation(st[0:TS, 4:5], st[0:TS, 4:5], ACT.Sqrt).then_inc(S["rms"], 1)
            for i in range(2):
                for h in range(IH):
                    k = i * IH + h
                    if k >= 3:
                        act.wait_ge(S["relu_used"], k - 2)
                    b = take(act, ("ix", i, h))
                    if k == 0:
                        evacuated(act, ("nout",))
                    give(nc.scalar.activation(relu[k % 3][:], b[:, 0:TP], ACT.Relu), ("ix", i, h))
                for h in range(AH):
                    k = i * AH + h
                    act.wait_ge(S["logit_done"], k + 1)
                    nc.scalar.activation(logit[k % 2][:], logit[k % 2][:], ACT.Exp, bias=st[:, k % 2:k % 2 + 1],
                                         accum_out=st[:, 2 + k % 2:3 + k % 2]).then_inc(S["exp_done"], 1)
                    b = take(act, ("aP", i, h))
                    nc.scalar.copy(probT[k % 2][:, 0:2, :], b[:, 0:2 * P].rearrange("p (n w) -> p n w", n=2))
                    give(nc.scalar.copy(probT[k % 2][0:META, 2, :], b[0:META, 2 * P:3 * P]), ("aP", i, h))
                    b = take(act, ("aO", i, h))
                    give(nc.scalar.copy(mixT[:, AH + h, P * i:P * i + P], b[:, 0:P]), ("aO", i, h))
            for q in range(SB):
                b = take(act, ("cki", q))
                if q >= 2:
                    evacuated(act, ("sI", q - 2))
                give(nc.scalar.copy(kiT[q % 2][:, 0:PAST], b[:, 0:PAST]), ("cki", q))
                b = take(act, ("sI", q))
                give(nc.scalar.activation(reluS[:, q, :], b[:, 0:KS], ACT.Relu), ("sI", q))
            act.wait_ge(S["m_sent"], 32)
            for q in range(SB):
                for n in range(4):
                    b = take(act, ("sK", q, n))
                    if q and n == 0:
                        take(act, ("sL", q - 1))
                    give(nc.scalar.copy(kT[:, 2 * n:2 * n + 2, :], b[:].rearrange("p (h t) -> p h t", h=2)), ("sK", q, n))
                act.wait_ge(S["logitS_done"], q + 1)
                nc.scalar.activation(logitS[q % 2][:], logitS[q % 2][:], ACT.Exp, bias=stS[:, q % 2:q % 2 + 1],
                                     accum_out=stS[:, 2 + q % 2:3 + q % 2]).then_inc(S["expS_done"], 1)
                b = take(act, ("sP", q))
                nc.scalar.copy(probS[q % 2][:, 0:2, :], b[:, 0:2 * AH * ST].rearrange("p (n w) -> p n w", n=2))
                give(nc.scalar.copy(probS[q % 2][0:ST, 2, :], b[0:ST, 2 * AH * ST:3 * AH * ST]), ("sP", q))
                b = take(act, ("sO", q))
                give(nc.scalar.copy(mixT[:, AH:2 * AH, SEQ + ST * q:SEQ + ST * (q + 1)], b[:, 0:AH * ST].rearrange("p (h t) -> p h t", h=AH)),
                     ("sO", q))
            tail_scalar(act, link, square_all, root, loop_copy)

        @block.gpsimd
        def _(pool):
            evacuated(pool, ("iw",))
            evacuated(pool, ("gcols",))
            nc.gpsimd.memset(mv_nat[:, :, :, DV:DV + 1], 1.0).then_inc(S["ones_set"], 1)
            evacuated(pool, ("nat", 3, 3))
            nc.gpsimd.memset(qz[:], 0.0).then_inc(S["qz_zero"], 1)
            evacuated(pool, ("nout",))
            nc.gpsimd.memset(iqz[:], 0.0)
            nc.gpsimd.memset(wz[:], 0.0).then_inc(S["iqz_zero"], 1)
            pool.wait_ge(S["iqz_done"], 1)
            pool.wait_ge(S["attn_done"], 1)
            nc.gpsimd.memset(qpad[:], 0.0).then_inc(S["qpad_zero"], 1)
            tail_pool(pool)

        @block.vector
        def _(dve):
            steps = [0]

            def link(ins):
                steps[0] += 1
                ins.then_inc(S["vec_step"], 1)
                dve.wait_ge(S["vec_step"], steps[0])

            def mean(key, turn, width):
                b = take(dve, key)
                give(nc.vector.tensor_scalar(rnorm[:, 0:width], b[:, 0:width], 1.0 / D, EPS, ALU.mult, ALU.add), key)
                dve.wait_ge(S["rnorm_sqrt"], turn + 1)
                nc.vector.reciprocal(rnorm[:, 0:width], rnorm[:, 0:width]).then_inc(S["rnorm_done"], 1)
                dve.wait_ge(S["rnorm_done"], turn + 1)

            def loop_copy(n, dst):
                first, iters, width = w_first[n], w_parts[n][2], dst.shape[2]
                def low(i, c):
                    dve.wait_ge(S["w_hi"], i * 4 + (split_from[n] + c + 1))
                    part = slice(P * (c % 2), P * (c % 2) + P)
                    nc.vector.tensor_tensor(wl[c // 2][:, :, part], wring[c // 2][:, :, part], wh[n][c % 2][:].bitcast(F32), ALU.subtract)\
                        .then_inc(S["w_lo"], 1)

                def copy_last(i, c):
                    dve.wait_ge(S["proj_mm"], (i + (first - 1)) * 4 + (5 + c))
                    nc.vector.tensor_copy(dst[:, bass.ds(i * 4 + (c - 4), 1), :], bank[c][:, 0:width].rearrange("p (a t) -> p a t", a=1))\
                        .then_inc(S["proj_hi"], 1)

                for c in range(4):
                    low(0, c)
                with dve.Fori(1, iters) as i:
                    for c in range(4):
                        low(i, c)
                        if c < 2:
                            copy_last(i, 2 + c)
                for c in range(2, 4):
                    copy_last(iters, c)

            dve.sem_inc(S["proj_hi"], 2)
            for i, (c, w) in enumerate(XTILES):
                for q in (0, 2):
                    b = take(dve, ("x", i, q))
                    give(nc.vector.tensor_copy(xT[:, 4 * q:4 * q + 4, c:c + w], b[:, 0:4 * w].rearrange("p (n w) -> p n w", n=4)), ("x", i, q))
            b = take(dve, ("gcols",))
            give(nc.vector.tensor_copy(gcol[:], b[:, 0:56]), ("gcols",))
            evacuated(dve, ("gcols",))
            for i in range(3):
                for q in range(4):
                    evacuated(dve, ("x", i, q))
            mean(("norm1",), 0, T)
            for c in range(KC):
                nc.vector.scalar_tensor_tensor(xnT[:, c, :], xT[:, c, :], gcol[:, c:c + 1], rnorm[:], ALU.mult, ALU.mult)\
                    .then_inc(S["xn_done"], 1)
            for k in range(KC):
                dve.wait_ge(S["xnh_done"], k + 1)
                nc.vector.tensor_tensor(xnl[:, k, :], xnT[:, k, :], xnh[:, k, :].bitcast(F32), ALU.subtract).then_inc(S["xnl_done"], 1)
            loop_copy(0, projT[:, 0:J_AQ, :])
            loop_copy(1, projT[:, J_AQ:NJ, :])
            b = take(dve, ("gate", 0))
            give(nc.vector.tensor_scalar(li[:], b[0:MH, 0:T], bi[:, 0:1], None, ALU.add), ("gate", 0))
            b = take(dve, ("gate", 1))
            give(nc.vector.tensor_scalar(mrow[:], b[0:MH, 0:T], bf[:, 0:1], None, ALU.add), ("gate", 1))
            evacuated(dve, ("gate", 1))
            link(nc.vector.tensor_scalar(tmp[:], mrow[:], -1.0, None, ALU.mult))
            nc.vector.tensor_tensor(tmp[:], tmp[:], mrow[:], ALU.max).then_inc(S["gates"], 1)
            dve.wait_ge(S["gates_ln"], 1)
            link(nc.vector.scalar_tensor_tensor(lf[:], mrow[:], 0.0, tmp[:], ALU.min, ALU.subtract))
            link(nc.vector.memset(tmp[:], 0.0))
            spans = [(0, TP, 0.0)] + [(TP + ST * q, ST, m0[:, q:q + 1]) for q in range(SB)]
            for c, w, start in spans:
                nc.vector.tensor_tensor_scan(bcum[:, c:c + w], lf[:, c:c + w], tmp[:, c:c + w], 0.0, ALU.add, ALU.add)
                ins = nc.vector.tensor_tensor_scan(mrow[:, c:c + w], lf[:, c:c + w], li[:, c:c + w], start, ALU.add, ALU.max)
            link(ins)
            link(nc.vector.tensor_tensor(rrow[:], bcum[:], mrow[:], ALU.subtract))
            nc.vector.tensor_tensor(crow[:], li[:], bcum[:], ALU.subtract)
            nc.vector.tensor_tensor(wrow[:, TP:T].rearrange("h (b t) -> h b t", t=ST), rrow[:, TP:T].rearrange("h (b t) -> h b t", t=ST),
                                    m0[:].rearrange("h (b a) -> h b a", a=1).to_broadcast([MH, SB, ST]), ALU.add).then_inc(S["rows_done"], 1)
            dve.wait_ge(S["ones_set"], 1)
            for i, (_, w) in enumerate(NAT):
                for q in (0, 1):
                    b = take(dve, ("nat", i, q))
                    give(nc.vector.tensor_copy(mv_nat[0:w, i, 2 * q:2 * q + 2, 0:DV], b[0:w, :].rearrange("p (h e) -> p h e", h=2)), ("nat", i, q))
                b = take(dve, ("nat", i, 6))
                give(nc.vector.tensor_scalar(mk_nat[0:w, i, :], b[0:w, :], scale_k, None, ALU.mult), ("nat", i, 6))
            b = take(dve, ("cols",))
            for j, (_, w) in enumerate(NAT):
                nc.vector.tensor_copy(ccol[0:w, j, :], b[0:w, MH * j:MH * j + MH])
            for j, (_, w) in enumerate(NTILES):
                ins = nc.vector.tensor_copy(ecol[0:w, j, :], b[0:w, 16 + MH * j:16 + MH * j + MH])
            give(ins, ("cols",))
            evacuated(dve, ("cols",))
            b = take(dve, ("wcol",))
            give(nc.vector.tensor_copy(wcol[:], b[:, 0:2 * IH].rearrange("p (i h) -> p i h", i=2)), ("wcol",))
            b = take(dve, ("n0",))
            give(nc.vector.tensor_copy(n0[:], b[:, 0:SB * MH].rearrange("p (b h) -> p b h", b=SB)), ("n0",))
            for n in range(2):
                b = take(dve, ("bias", n))
                give(nc.vector.tensor_copy(brow[:, n * (RW // 2):(n + 1) * (RW // 2)], b[0:AH, 0:RW // 2]), ("bias", n))

            def head_output(b, rows_, i, e, turn, key, ht):
                s0, s1, s2 = (st[0:rows_, n + i:n + i + 1] for n in (0, 2, 4))
                link(nc.vector.tensor_scalar(s1, b[0:rows_, DV:DV + 1], -1.0, None, ALU.mult))
                link(nc.vector.tensor_tensor(s0, s1, b[0:rows_, DV:DV + 1], ALU.max))
                link(nc.vector.tensor_tensor(s1, s0, e, ALU.max))
                link(nc.vector.reciprocal(s0, s1))
                give(nc.vector.tensor_scalar(ht[0:rows_, :], b[0:rows_, 0:DV], s0, None, ALU.mult), key)
                evacuated(dve, key)
                link(nc.vector.tensor_tensor_reduce(cout[0:rows_, :], ht[0:rows_, :], ht[0:rows_, :], 1.0, 0.0, ALU.mult, ALU.add, s2))
                nc.vector.tensor_scalar(s2, s2, 1.0 / DV, EPS, ALU.mult, ALU.add).then_inc(S["ssq"], 1)
                dve.wait_ge(S["rms"], turn)
                link(nc.vector.reciprocal(s0, s2))
                nc.vector.tensor_scalar(ht[0:rows_, :], ht[0:rows_, :], s0, None, ALU.mult).then_inc(S["hn"], 1)

            def mix_in(b, h, width, col, key):
                for c in range(2):
                    ins = nc.vector.scalar_tensor_tensor(mixT[:, 2 * h + c, col:col + width], b[:, c * width:(c + 1) * width], gcol[:, 48 + 2 * h + c:49 + 2 * h + c],
                                                         projT[:, J_MO + 2 * h + c, META + col:META + col + width], ALU.mult, ALU.mult)
                give(ins, key)

            for n in range(2):
                dve.wait_ge(S[f"natk_sent{n}"], 64)
            dve.wait_ge(S["ki_sent"], 64)
            dve.wait_ge(S["row_sent"], 16)
            dve.wait_ge(S["act_step"], 1)
            mask = const("decay_p")
            for h in range(MH):
                b = take(dve, ("mR", h))
                if h:
                    take(dve, ("mC", h - 1))
                for j in range(3):
                    w = NAT[j][1]
                    ins = nc.vector.scalar_tensor_tensor(decay[0:w, j, :], b[0:w, 0:SEQ], ccol[0:w, j, h:h + 1],
                                                         mask[0:w, j * SEQ:(j + 1) * SEQ], ALU.add, ALU.add)
                give(ins, ("mR", h))
                dve.wait_ge(S["decay_done"], h + 1)
                for j in range(3):
                    w = NAT[j][1]
                    b = take(dve, ("mS", h, j))
                    give(nc.vector.scalar_tensor_tensor(gated[0:w, j, :], b[0:w, 0:SEQ], scale_k, decay[0:w, j, :], ALU.mult, ALU.mult), ("mS", h, j))
                for j in range(3):
                    w = NAT[j][1]
                    ins = nc.vector.tensor_scalar(kw[0:w, j, :], mk_nat[0:w, j, h * DK:(h + 1) * DK], decay[0:w, j, SEQ - 1:SEQ], None, ALU.mult)
                ins.then_inc(S["kw_done"], 1)
                if h:
                    dve.wait_ge(S["cout_sent"], 16 * h)
                for i in range(2):
                    b = take(dve, ("mN", h, i))
                    head_output(b, P, i, ecol[:, i, h:h + 1], 2 * h + i + 1, ("mN", h, i), hnorm[i])
                b = take(dve, ("mC", h))
                link(nc.vector.tensor_copy(cout[:], b[:, 0:DV]))
                give(nc.vector.tensor_copy(npr[:, h:h + 1], b[:, DV:DV + 1]), ("mC", h))
                for i in range(2):
                    mix_in(take(dve, ("mT", h, i)), h, P, P * i, ("mT", h, i))
            dve.wait_ge(S["cout_sent"], 16 * MH)
            dve.wait_ge(S["qz_zero"], 1)
            n_block = lambda tile: tile[:].rearrange("p (b x) -> p b x", x=TS + ST)[:, :, 0:ST]
            for h in range(MH):
                s = h % 2
                b = take(dve, ("sR", h))
                give(nc.vector.scalar_tensor_tensor(decay[0:TS, 0, 0:TS], b[0:TS, 0:TS], ccol[0:TS, 3, h:h + 1], const("decay_s"), ALU.add, ALU.add), ("sR", h))
                b = take(dve, ("sW", h))
                nc.vector.tensor_copy(abc[:], b[:, 0:TS].rearrange("p (b t) -> p b t", t=ST)[:, :, ST - 1])
                if h >= 2:
                    dve.wait_ge(S[f"c_in{s}"], 16 * (h // 2 + 1))
                nc.vector.tensor_copy(C0[s][:, :, DV], n0[:, :, h])
                ins = nc.vector.tensor_tensor(n_block(qz), projT[:, J_MQ + h, TP:T].rearrange("p (b t) -> p b t", t=ST),
                                              b[:, 0:TS].rearrange("p (b t) -> p b t", t=ST), ALU.mult)
                give(ins, ("sW", h))
                dve.wait_ge(S["decay_done"], MH + h + 1)
                b = take(dve, ("sS", h))
                give(nc.vector.scalar_tensor_tensor(gated[0:TS, 0, 0:TS], b[0:TS, 0:TS], scale_k, decay[0:TS, 0, 0:TS], ALU.mult, ALU.mult), ("sS", h))
                for q in range(SB):
                    ins = nc.vector.tensor_scalar(kwz[:, q, :], mk_nat[0:TS, 3, h * DK:(h + 1) * DK],
                                                  decay[0:TS, 0, ST * q + ST - 1:ST * q + ST], None, ALU.mult)
                ins.then_inc(S["kwz_done"], 1)
                b = take(dve, ("sN", h))
                head_output(b, TS, 0, ecol[0:TS, 2, h:h + 1], 2 * MH + h + 1, ("sN", h), hnorm[0])
                mix_in(take(dve, ("sT", h)), h, TS, SEQ, ("sT", h))
                for q in range(SB):
                    b = take(dve, ("sC", h, q))
                    give(nc.vector.scalar_tensor_tensor(C0[s][:, q, :], C0[s][:, q, :], abc[:, q:q + 1], b[:, 0:DV + 1], ALU.mult, ALU.add), ("sC", h, q))
                evacuated(dve, ("sC", h, SB - 1))
                nc.vector.tensor_copy(nsa[:].rearrange("p (b h) -> p b h", b=SB)[:, :, h], C0[s][:, :, DV]).then_inc(S["nsa_done"], 1)
            b = take(dve, ("nout",))
            nc.vector.tensor_copy(nrow[0:MH, :], b[0:MH, 0:P])
            give(nc.vector.tensor_copy(nout[:], b[0:SB * MH, P:2 * P]), ("nout",))

            for h in range(AH):
                b = take(dve, ("bt", h))
                give(nc.vector.tensor_copy(bt[:, h, :], b[:, 0:BTW]), ("bt", h))
            b = take(dve, ("bs",))
            give(nc.vector.tensor_copy(biasS[:], b[0:AH * ST, 0:KS]), ("bs",))
            for i in range(2):
                for h in range(IH):
                    evacuated(dve, ("ix", i, h))
                    k = i * IH + h
                    if h == 0:
                        ins = nc.vector.tensor_scalar(score[:], relu[k % 3][:], wcol[:, i, 0:1], None, ALU.mult)
                    else:
                        ins = nc.vector.scalar_tensor_tensor(score[:], relu[k % 3][:], wcol[:, i, h:h + 1], score[:], ALU.mult, ALU.add)
                    ins.then_inc(S["relu_used"], 1)
                    dve.wait_ge(S["relu_used"], k + 1)
                causal = const("causal_p")[:, i * TP:(i + 1) * TP]
                link(nc.vector.tensor_tensor(score[:], score[:], causal, ALU.add))
                for _ in range(TOPK_P // 8):
                    link(nc.vector.max(top8[:], score[:]))
                    link(nc.vector.match_replace(score[:], top8[:], score[:], GONE))
                link(nc.vector.tensor_scalar(keep[:], score[:], -2.0e38, NEG, ALU.is_gt, ALU.mult))
                link(nc.vector.tensor_tensor(keep[:], keep[:], causal, ALU.add))
                for h in range(AH + 1):
                    if h < AH:
                        k = i * AH + h
                        if k >= 2:
                            take(dve, ("aP", (k - 2) // AH, (k - 2) % AH))
                        b = take(dve, ("aL", i, h))
                        give(nc.vector.scalar_tensor_tensor(logit[k % 2][:], b[:, 0:TP], scale_a, bt[:, h, P - P * i:P - P * i + TP], ALU.mult, ALU.add), ("aL", i, h))
                        evacuated(dve, ("aL", i, h))
                        link(nc.vector.tensor_tensor(logit[k % 2][:], logit[k % 2][:], keep[:], ALU.add))
                        nc.vector.tensor_reduce(st[:, k % 2:k % 2 + 1], logit[k % 2][:], AX_X, ALU.max, negate=True).then_inc(S["logit_done"], 1)
                    if h:
                        k = i * AH + h - 1
                        dve.wait_ge(S["exp_done"], k + 1)
                        link(nc.vector.reciprocal(st[:, 4 + k % 2:5 + k % 2], st[:, 2 + k % 2:3 + k % 2]))
                        nc.vector.tensor_scalar(logit[k % 2][:], logit[k % 2][:], st[:, 4 + k % 2:5 + k % 2], None, ALU.mult).then_inc(S["prob_done"], 1)
            dve.wait_ge(S["iqz_zero"], 1)
            for e in range(2):
                rows_ = slice(ID * e, ID * e + ID)
                for c in range(IH // 2):
                    ins = nc.vector.tensor_copy(iqz[rows_, :, (2 * c + e) * ST:(2 * c + e + 1) * ST],
                                                projT[rows_, J_IQ + c, TP:T].rearrange("p (b t) -> p b t", t=ST))
            ins.then_inc(S["iqz_done"], 1)
            b = take(dve, ("wrep",))
            give(nc.vector.tensor_tensor(n_block(wz), b[:, 0:TS].rearrange("p (b t) -> p b t", t=ST),
                                         const("same_t").rearrange("p (b t) -> p b t", t=ST), ALU.mult), ("wrep",))
            take(dve, ("aO", 1, AH - 1))
            evacuated(dve, ("wrep",))
            dve.sem_inc(S["wz_done"], 1)
            dve.sem_inc(S["attn_done"], 1)
            dve.wait_ge(S["v_sent"], 64)
            b = take(dve, ("sScore",))
            give(nc.vector.tensor_tensor(scoreS[:], b[0:TS, 0:KS], const("causal_s"), ALU.add), ("sScore",))
            evacuated(dve, ("sScore",))
            left = TOPK_S
            while left > 0:
                link(nc.vector.max(top8S[:], scoreS[:]))
                if left < 8:
                    link(nc.vector.memset(top8S[:, left:8], GONE))
                link(nc.vector.match_replace(scoreS[:], top8S[:], scoreS[:], GONE))
                left -= 8
            link(nc.vector.tensor_scalar(keepS[:], scoreS[:], -2.0e38, NEG, ALU.is_gt, ALU.mult))
            nc.vector.tensor_tensor(keepS[:], keepS[:], const("causal_s"), ALU.add).then_inc(S["keepS_done"], 1)
            dve.wait_ge(S["qpad_zero"], 1)
            for h in range(AH):
                ins = nc.vector.tensor_copy(qpad[:, :, (TS + ST) * h:(TS + ST) * h + ST], projT[:, J_AQ + h, TP:T].rearrange("p (b t) -> p b t", t=ST))
            ins.then_inc(S["qpad_done"], 1)
            for q in range(SB + 1):
                if q < SB:
                    if q >= 2:
                        take(dve, ("sP", q - 2))
                    b = take(dve, ("sL", q))
                    give(nc.vector.scalar_tensor_tensor(logitS[q % 2][:], b[0:AH * ST, 0:KS], scale_a, biasS[:], ALU.mult, ALU.add), ("sL", q))
                    evacuated(dve, ("sL", q))
                    nc.vector.tensor_reduce(stS[:, q % 2:q % 2 + 1], logitS[q % 2][:], AX_X, ALU.max, negate=True).then_inc(S["logitS_done"], 1)
                    dve.wait_ge(S["expS_done"], q + 1)
                    link(nc.vector.reciprocal(top8S[:, 0:1], stS[:, 2 + q % 2:3 + q % 2]))
                    nc.vector.tensor_scalar(logitS[q % 2][:], logitS[q % 2][:], top8S[:, 0:1], None, ALU.mult).then_inc(S["probS_done"], 1)
            tail_vector(dve, link, mean, loop_copy)


INS = ["x_prompt", "x_sample", "cache_k", "cache_v", "cache_kidx", "state_C", "state_n", "state_m", "page_table",
       "meta_tokens", "rel_bias", "final_norm_g", "norm1_g", "w_in", "b_i", "b_f", "mh_norm_g", "w_out", "norm2_g",
       "peer_wq", "peer_k1", "peer_k2", "peer_u", "peer_v"]
OUTS = [("y_prompt", (1, SEQ, D)), ("y_sample", (SB, ST, D)),
        ("k_prompt", (1, 1, TP, AH, DH)), ("v_prompt", (1, 1, TP, AH, DH)), ("kidx_prompt", (1, 1, TP, ID)),
        ("C_prompt", (1, 1, MH, DK, DV)), ("n_prompt", (1, 1, MH, DK)), ("m_prompt", (1, 1, MH)),
        ("k_sample", (1, SB, ST, AH, DH)), ("v_sample", (1, SB, ST, AH, DH)), ("kidx_sample", (1, SB, ST, ID)),
        ("C_sample", (1, SB, MH, DK, DV)), ("n_sample", (1, SB, MH, DK)), ("m_sample", (1, SB, MH))]


def kernel(**inputs):
    import concourse.bacc as bacc
    from concourse.bass_utils import run_bass_kernel_spmd

    nc = bacc.Bacc("TRN2", target_bir_lowering=False, num_devices=1)
    arrays, a, o = {}, {}, {}
    for name in INS:
        arrays[f"in_{name}"] = np.ascontiguousarray(inputs[name])
        dt = mybir.dt.from_np(arrays[f"in_{name}"].dtype)
        a[name] = nc.dram_tensor(f"in_{name}", arrays[f"in_{name}"].shape, dt, kind="ExternalInput").ap()
    for name, shape in OUTS:
        o[name] = nc.dram_tensor(f"out_{name}", shape, F32, kind="ExternalOutput").ap()
    const_at, packed = constants()
    arrays["in_constants"] = packed
    consts = nc.dram_tensor("in_constants", packed.shape, F32, kind="ExternalInput").ap()
    build(nc, a, o, consts, const_at)
    r = run_bass_kernel_spmd(nc, [arrays], core_ids=[0])
    return tuple(r.results[0][f"out_{name}"] for name, _ in OUTS)
```
